# Optimizing a Trainium2 kernel written in Bass

```python
import math
import jax, jax.numpy as jnp
from jax import lax
import numpy as np

D_MODEL = 1024
BATCH = 1
SEQ = 1024
DEPTH = 2

GRID_W = 64
CTX_LEN = 256
N_MIXERS = 4
Q_BLOCK = 128
NORM_EPS = 1e-6
NEG_INF = -1e30
ROPE_BASE = 10000.0
ROPE_DIM = 64

MLA_HEADS = 8
MLA_Q_RANK = 384
MLA_KV_RANK = 256
MLA_NOPE = 128
MLA_ROPE = ROPE_DIM
MLA_V = 128
MLA_WIDTH = MLA_HEADS * MLA_V

HY_WIDTH = D_MODEL
HY_ORDER = 2
HY_SHORT = 3
HY_EMB = 33
HY_BANDS = (HY_EMB - 1) // 2
HY_FILT_HIDDEN = 64
HY_DECAY_TARGET = 1e-2
HY_FAST_DECAY = 0.3
HY_SLOW_DECAY = 1.5

SWA_Q_HEADS = 16
SWA_KV_HEADS = 4
SWA_GROUP = SWA_Q_HEADS // SWA_KV_HEADS
SWA_HEAD_DIM = ROPE_DIM
SWA_WINDOW = 128
SWA_WIDTH = SWA_Q_HEADS * SWA_HEAD_DIM

CF_WIDTH = D_MODEL
CF_KERNEL = 31


def n_layers_of(m):
    return len(range(m, DEPTH, N_MIXERS))

def rmsnorm(x, g):
    xf = x.astype(jnp.float32)
    y = xf * lax.rsqrt(jnp.mean(xf * xf, axis=-1, keepdims=True) + NORM_EPS)
    return (y * g.astype(jnp.float32)).astype(x.dtype)

def layernorm(x, g, b):
    xf = x.astype(jnp.float32)
    mu = jnp.mean(xf, axis=-1, keepdims=True)
    xc = xf - mu
    var = jnp.mean(xc * xc, axis=-1, keepdims=True)
    return (xc * lax.rsqrt(var + NORM_EPS) * g.astype(jnp.float32) + b.astype(jnp.float32)).astype(x.dtype)

def modulate(h, shift, scale):
    return h * (1 + scale) + shift

def grid_rope(L, dim, dtype):
    rows = L // GRID_W
    row = jnp.repeat(jnp.arange(rows, dtype=jnp.float32), GRID_W)
    col = jnp.tile(jnp.arange(GRID_W, dtype=jnp.float32), rows)
    n_freq = dim // 4
    inv = ROPE_BASE ** (-jnp.arange(n_freq, dtype=jnp.float32) / n_freq)
    ang = jnp.concatenate([row[:, None] * inv, col[:, None] * inv], axis=-1)
    return jnp.cos(ang).astype(dtype), jnp.sin(ang).astype(dtype)

def apply_rope(x, cos, sin):
    half = x.shape[-1] // 2
    x1, x2 = x[..., :half], x[..., half:]
    return jnp.concatenate([x1 * cos - x2 * sin, x1 * sin + x2 * cos], axis=-1)

def depthwise_conv(u, w, b):
    K, C = w.shape
    pad = (K - 1) // 2
    y = lax.conv_general_dilated(u, w[:, None, :].astype(u.dtype), window_strides=(1,),
                                 padding=[(pad, pad)], dimension_numbers=('NWC', 'WIO', 'NWC'),
                                 feature_group_count=C)
    return y + b

def to_blocks(t):
    B, L = t.shape[:2]
    return jnp.moveaxis(t.reshape(B, L // Q_BLOCK, Q_BLOCK, *t.shape[2:]), 1, 0)

def from_blocks(o):
    nb, B, Q = o.shape[:3]
    return jnp.moveaxis(o, 0, 1).reshape(B, nb * Q, *o.shape[3:])

def mla_mixer(a, ac, cos, sin, w_in, q_norm_g, kv_norm_g, w_uq, w_ukv, w_out, ctx_out):
    B, L, _ = a.shape
    splits = [MLA_Q_RANK, MLA_Q_RANK + MLA_KV_RANK, MLA_Q_RANK + MLA_KV_RANK + MLA_ROPE]

    def project(t):
        n = t.shape[1]
        cq, ckv, k_rope, gate = jnp.split(t @ w_in, splits, axis=-1)
        q = (rmsnorm(cq, q_norm_g) @ w_uq).reshape(B, n, MLA_HEADS, MLA_NOPE + MLA_ROPE)
        kv = (rmsnorm(ckv, kv_norm_g) @ w_ukv).reshape(B, n, MLA_HEADS, MLA_NOPE + MLA_V)
        return q[..., :MLA_NOPE], q[..., MLA_NOPE:], kv[..., :MLA_NOPE], k_rope, kv[..., MLA_NOPE:], gate

    qn, qr, kn, kr, v, gate = project(a)
    qr = apply_rope(qr, cos[:, None, :], sin[:, None, :])
    kr = apply_rope(kr, cos, sin)
    qnc, qrc, knc, krc, vc, gatec = project(ac)
    scale = (MLA_NOPE + MLA_ROPE) ** -0.5

    def scores(qn_, qr_, kn_, kr_):
        s = jnp.einsum('bqhd,bkhd->bhqk', qn_, kn_) + jnp.einsum('bqhr,bkr->bhqk', qr_, kr_)
        return s.astype(jnp.float32) * scale

    def attend(blk):
        qn_b, qr_b = blk
        s = jnp.concatenate([scores(qn_b, qr_b, kn, kr), scores(qn_b, qr_b, knc, krc)], axis=-1)
        p = jax.nn.softmax(s, axis=-1).astype(v.dtype)
        return (jnp.einsum('bhqk,bkhd->bqhd', p[..., :L], v)
                + jnp.einsum('bhqk,bkhd->bqhd', p[..., L:], vc))

    o = from_blocks(lax.map(attend, (to_blocks(qn), to_blocks(qr)))).reshape(B, L, MLA_WIDTH)
    y = (o * jax.nn.silu(gate)) @ w_out
    yc = None
    if ctx_out:
        pc = jax.nn.softmax(scores(qnc, qrc, knc, krc), axis=-1).astype(vc.dtype)
        oc = jnp.einsum('bhqk,bkhd->bqhd', pc, vc).reshape(B, -1, MLA_WIDTH)
        yc = (oc * jax.nn.silu(gatec)) @ w_out
    return y, yc

def hyena_filter_spectra(L, w_in, w_hid, b, freq, w_out):
    f32 = jnp.float32
    t = jnp.linspace(0.0, 1.0, L, dtype=f32)[:, None]
    wpos = (2.0 * math.pi / L) * jnp.arange(L, dtype=f32)[:, None]
    bands = jnp.linspace(1e-4, HY_BANDS - 1, HY_BANDS, dtype=f32)[None, :]
    hdn = jnp.concatenate([t, jnp.cos(bands * wpos), -jnp.sin(bands * wpos)], axis=-1)
    b, freq = b.astype(f32), freq.astype(f32)
    for k, w in enumerate((w_in, w_hid[0], w_hid[1])):
        hdn = jnp.sin(freq[k] * (hdn @ w.astype(f32) + b[k]))
    h = (hdn @ w_out.astype(f32)).reshape(L, HY_ORDER, 2, HY_WIDTH)
    deltas = jnp.abs(jnp.linspace(math.log(HY_DECAY_TARGET) / HY_FAST_DECAY,
                                  math.log(HY_DECAY_TARGET) / HY_SLOW_DECAY, HY_WIDTH, dtype=f32))
    h = h * jnp.exp(-t * deltas)[:, None, None, :]
    hf, hb = h[:, :, 0], h[:, :, 1]
    k_circ = jnp.concatenate([hf[:1] + hb[:1], hf[1:], jnp.zeros_like(hf[:1]), hb[:0:-1]], axis=0)
    return jnp.fft.rfft(k_circ, axis=0)

def fft_long_conv(u, spec):
    L = u.shape[1]
    U = jnp.fft.rfft(u.astype(jnp.float32), n=2 * L, axis=1)
    return jnp.fft.irfft(U * spec, n=2 * L, axis=1)[:, :L].astype(u.dtype)

def hyena_seq(t, w_in, conv_w, conv_b, spec, bias, w_out):
    u, gate = jnp.split(t @ w_in, [(HY_ORDER + 1) * HY_WIDTH], axis=-1)
    u = depthwise_conv(u, conv_w, conv_b)
    v, *gates = jnp.split(u, HY_ORDER + 1, axis=-1)
    z = v
    for o in range(HY_ORDER):
        z = gates[o] * (fft_long_conv(z, spec[:, o]) + z * bias[o])
    return (z * jax.nn.silu(gate)) @ w_out

def swa_mixer(a, ac, cos, sin, w_in, sink, w_out, ctx_out):
    B, L, _ = a.shape
    nq = SWA_Q_HEADS * SWA_HEAD_DIM
    nkv = SWA_KV_HEADS * SWA_HEAD_DIM

    def project(t):
        n = t.shape[1]
        q, k, v, gate = jnp.split(t @ w_in, [nq, nq + nkv, nq + 2 * nkv], axis=-1)
        return (q.reshape(B, n, SWA_KV_HEADS, SWA_GROUP, SWA_HEAD_DIM),
                k.reshape(B, n, SWA_KV_HEADS, SWA_HEAD_DIM),
                v.reshape(B, n, SWA_KV_HEADS, SWA_HEAD_DIM), gate)

    q, k, v, gate = project(a)
    q = apply_rope(q, cos[:, None, None, :], sin[:, None, None, :])
    k = apply_rope(k, cos[:, None, :], sin[:, None, :])
    qc, kc, vc, gatec = project(ac)
    scale = SWA_HEAD_DIM ** -0.5
    sink_logit = sink.astype(jnp.float32).reshape(SWA_KV_HEADS, SWA_GROUP, 1, 1)

    def softmax_with_sink(parts, n_q):
        s_sink = jnp.broadcast_to(sink_logit, (B, SWA_KV_HEADS, SWA_GROUP, n_q, 1))
        p = jax.nn.softmax(jnp.concatenate([*parts, s_sink], axis=-1), axis=-1)
        return p[..., :-1].astype(v.dtype)

    span = Q_BLOCK + 2 * SWA_WINDOW
    pad = ((0, 0), (SWA_WINDOW, SWA_WINDOW), (0, 0), (0, 0))
    kp, vp = jnp.pad(k, pad), jnp.pad(v, pad)
    rel = jnp.arange(span)[None, :] - jnp.arange(Q_BLOCK)[:, None]
    band = (rel >= 0) & (rel <= 2 * SWA_WINDOW)

    def attend(args):
        j, q_b = args
        start = j * Q_BLOCK
        k_b = lax.dynamic_slice_in_dim(kp, start, span, axis=1)
        v_b = lax.dynamic_slice_in_dim(vp, start, span, axis=1)
        kpos = start - SWA_WINDOW + jnp.arange(span)
        valid = band & ((kpos >= 0) & (kpos < L))[None, :]
        s_win = jnp.einsum('bqhgd,bkhd->bhgqk', q_b, k_b).astype(jnp.float32) * scale
        s_win = jnp.where(valid, s_win, NEG_INF)
        s_ctx = jnp.einsum('bqhgd,bkhd->bhgqk', q_b, kc).astype(jnp.float32) * scale
        p = softmax_with_sink([s_win, s_ctx], Q_BLOCK)
        return (jnp.einsum('bhgqk,bkhd->bqhgd', p[..., :span], v_b)
                + jnp.einsum('bhgqk,bkhd->bqhgd', p[..., span:], vc))

    o = from_blocks(lax.map(attend, (jnp.arange(L // Q_BLOCK), to_blocks(q)))).reshape(B, L, SWA_WIDTH)
    y = (o * jax.nn.silu(gate)) @ w_out
    yc = None
    if ctx_out:
        s = jnp.einsum('bqhgd,bkhd->bhgqk', qc, kc).astype(jnp.float32) * scale
        pc = softmax_with_sink([s], qc.shape[1])
        oc = jnp.einsum('bhgqk,bkhd->bqhgd', pc, vc).reshape(B, -1, SWA_WIDTH)
        yc = (oc * jax.nn.silu(gatec)) @ w_out
    return y, yc

def conformer_seq(t, w_in, dw_w, dw_b, ln_g, ln_b, w_out):
    a, b, gate = jnp.split(t @ w_in, 3, axis=-1)
    u = a * jax.nn.sigmoid(b)
    u = depthwise_conv(u, dw_w, dw_b)
    u = jax.nn.silu(layernorm(u, ln_g, ln_b))
    return (u * jax.nn.silu(gate)) @ w_out

def first_inputs(seed: int = 0) -> dict:
    key = jax.random.key(seed)
    ks = iter(jax.random.split(key, 40))
    D = D_MODEL
    f32 = jnp.float32

    def nrm(shape, std):
        return jax.random.normal(next(ks), shape, f32) * std

    def gain(shape):
        return 1.0 + nrm(shape, 0.02)

    nA, nB, nC, nD = (n_layers_of(m) for m in range(N_MIXERS))
    mla_in = MLA_Q_RANK + MLA_KV_RANK + MLA_ROPE + MLA_WIDTH
    swa_in = SWA_Q_HEADS * SWA_HEAD_DIM + 2 * SWA_KV_HEADS * SWA_HEAD_DIM + SWA_WIDTH
    return {
        "x": nrm((BATCH, SEQ, D), 1.0),
        "c": nrm((BATCH, D), 1.0),
        "ctx": nrm((BATCH, CTX_LEN, D), 1.0),
        "c_ctx": nrm((D,), 1.0),
        "norm_g": gain((DEPTH, D)),
        "ada_w": nrm((DEPTH, D, 3 * D), 0.5 * D ** -0.5),
        "ada_b": nrm((DEPTH, 3 * D), 0.02),
        "final_g": gain((D,)),
        "mla_w_in": nrm((nA, D, mla_in), D ** -0.5),
        "mla_q_norm_g": gain((nA, MLA_Q_RANK)),
        "mla_kv_norm_g": gain((nA, MLA_KV_RANK)),
        "mla_w_uq": nrm((nA, MLA_Q_RANK, MLA_HEADS * (MLA_NOPE + MLA_ROPE)), MLA_Q_RANK ** -0.5),
        "mla_w_ukv": nrm((nA, MLA_KV_RANK, MLA_HEADS * (MLA_NOPE + MLA_V)), MLA_KV_RANK ** -0.5),
        "mla_w_out": nrm((nA, MLA_WIDTH, D), MLA_WIDTH ** -0.5),
        "hy_w_in": nrm((nB, D, (HY_ORDER + 2) * HY_WIDTH), D ** -0.5),
        "hy_conv_w": nrm((nB, HY_SHORT, (HY_ORDER + 1) * HY_WIDTH), HY_SHORT ** -0.5),
        "hy_conv_b": nrm((nB, (HY_ORDER + 1) * HY_WIDTH), 0.02),
        "hy_filt_w_in": nrm((nB, HY_EMB, HY_FILT_HIDDEN), HY_EMB ** -0.5),
        "hy_filt_w_hid": nrm((nB, 2, HY_FILT_HIDDEN, HY_FILT_HIDDEN), HY_FILT_HIDDEN ** -0.5),
        "hy_filt_b": nrm((nB, 3, HY_FILT_HIDDEN), 0.2),
        "hy_filt_freq": gain((nB, 3, HY_FILT_HIDDEN)),
        "hy_filt_w_out": nrm((nB, HY_FILT_HIDDEN, HY_ORDER * 2 * HY_WIDTH), 0.005),
        "hy_bias": nrm((nB, HY_ORDER, HY_WIDTH), 0.5),
        "hy_w_out": nrm((nB, HY_WIDTH, D), HY_WIDTH ** -0.5),
        "swa_w_in": nrm((nC, D, swa_in), D ** -0.5),
        "swa_sink": nrm((nC, SWA_Q_HEADS), 0.5),
        "swa_w_out": nrm((nC, SWA_WIDTH, D), SWA_WIDTH ** -0.5),
        "cf_w_in": nrm((nD, D, 3 * CF_WIDTH), D ** -0.5),
        "cf_dw_w": nrm((nD, CF_KERNEL, CF_WIDTH), CF_KERNEL ** -0.5),
        "cf_dw_b": nrm((nD, CF_WIDTH), 0.02),
        "cf_ln_g": gain((nD, CF_WIDTH)),
        "cf_ln_b": nrm((nD, CF_WIDTH), 0.02),
        "cf_w_out": nrm((nD, CF_WIDTH, D), CF_WIDTH ** -0.5),
    }

def first_block(x, c, ctx, c_ctx, norm_g, ada_w, ada_b, final_g,
              mla_w_in, mla_q_norm_g, mla_kv_norm_g, mla_w_uq, mla_w_ukv, mla_w_out,
              hy_w_in, hy_conv_w, hy_conv_b, hy_filt_w_in, hy_filt_w_hid, hy_filt_b, hy_filt_freq,
              hy_filt_w_out, hy_bias, hy_w_out,
              swa_w_in, swa_sink, swa_w_out,
              cf_w_in, cf_dw_w, cf_dw_b, cf_ln_g, cf_ln_b, cf_w_out):
    B, L, _ = x.shape
    Lc = ctx.shape[1]
    cos, sin = grid_rope(L, ROPE_DIM, x.dtype)
    silu_c = jax.nn.silu(c)
    silu_cc = jax.nn.silu(c_ctx)
    xc = ctx
    for i in range(DEPTH):
        m, j = i % N_MIXERS, i // N_MIXERS
        ctx_out = i < DEPTH - 1
        shift, scale, gate = jnp.split((silu_c @ ada_w[i] + ada_b[i])[:, None, :], 3, axis=-1)
        a = modulate(rmsnorm(x, norm_g[i]), shift, scale)
        if ctx_out or m in (0, 2):
            shift_c, scale_c, gate_c = jnp.split(silu_cc @ ada_w[i] + ada_b[i], 3, axis=-1)
            ac = modulate(rmsnorm(xc, norm_g[i]), shift_c, scale_c)
        yc = None
        if m == 0:
            y, yc = mla_mixer(a, ac, cos, sin, mla_w_in[j], mla_q_norm_g[j], mla_kv_norm_g[j],
                              mla_w_uq[j], mla_w_ukv[j], mla_w_out[j], ctx_out)
        elif m == 1:
            filt = (hy_filt_w_in[j], hy_filt_w_hid[j], hy_filt_b[j], hy_filt_freq[j], hy_filt_w_out[j])
            y = hyena_seq(a, hy_w_in[j], hy_conv_w[j], hy_conv_b[j],
                          hyena_filter_spectra(L, *filt), hy_bias[j], hy_w_out[j])
            if ctx_out:
                yc = hyena_seq(ac, hy_w_in[j], hy_conv_w[j], hy_conv_b[j],
                               hyena_filter_spectra(Lc, *filt), hy_bias[j], hy_w_out[j])
        elif m == 2:
            y, yc = swa_mixer(a, ac, cos, sin, swa_w_in[j], swa_sink[j], swa_w_out[j], ctx_out)
        else:
            y = conformer_seq(a, cf_w_in[j], cf_dw_w[j], cf_dw_b[j], cf_ln_g[j], cf_ln_b[j], cf_w_out[j])
            if ctx_out:
                yc = conformer_seq(ac, cf_w_in[j], cf_dw_w[j], cf_dw_b[j], cf_ln_g[j], cf_ln_b[j], cf_w_out[j])
        x = x + gate * y
        if ctx_out:
            xc = xc + gate_c * yc
    return rmsnorm(x, final_g)


DEPTH_2 = 1

N_Q_HEADS = 8
N_KV_HEADS = 2
GROUP = N_Q_HEADS // N_KV_HEADS
HEAD_DIM = 64
ROT_DIM = HEAD_DIM // 4
ROPE_THETA = 500000.0
WINDOW = 128
ATTN_BLOCK = 128
ATTN_WIDTH = N_Q_HEADS * HEAD_DIM
KV_WIDTH = N_KV_HEADS * HEAD_DIM

HGRN_HEADS = 4
HGRN_KEY_DIM = 128
HGRN_VAL_DIM = 128
HGRN_KEY_WIDTH = HGRN_HEADS * HGRN_KEY_DIM
HGRN_WIDTH = HGRN_HEADS * HGRN_VAL_DIM
HGRN_CHUNK = 64

IN_SIZES = (ATTN_WIDTH, KV_WIDTH, KV_WIDTH,
            HGRN_KEY_WIDTH, HGRN_KEY_WIDTH, HGRN_WIDTH, HGRN_WIDTH,
            D_MODEL, D_MODEL)
IN_WIDTH = sum(IN_SIZES)

N_GROUPS = 4
EXPERTS_PER_GROUP = 8
N_EXPERTS = N_GROUPS * EXPERTS_PER_GROUP
TOP_K = 2
EXPERT_FF = 512
MOE_BLOCK = 128


def rms_norm(x, w):
    xf = x.astype(jnp.float32)
    y = xf * lax.rsqrt(jnp.mean(xf * xf, axis=-1, keepdims=True) + NORM_EPS)
    return (y * w.astype(jnp.float32)).astype(x.dtype)

def rope_tables(positions):
    inv_freq = ROPE_THETA ** (-jnp.arange(0, ROT_DIM, 2, dtype=jnp.float32) / ROT_DIM)
    ang = positions.astype(jnp.float32)[..., None] * inv_freq
    return jnp.cos(ang)[:, :, None, :], jnp.sin(ang)[:, :, None, :]

def partial_rope(x, cos, sin):
    half = ROT_DIM // 2
    xf = x.astype(jnp.float32)
    x1, x2 = xf[..., :half], xf[..., half:ROT_DIM]
    out = jnp.concatenate([x1 * cos - x2 * sin, x2 * cos + x1 * sin, xf[..., ROT_DIM:]], axis=-1)
    return out.astype(x.dtype)

def sliding_window_gqa(q, k, v, sinks):
    B, S = q.shape[0], q.shape[1]
    nb = S // ATTN_BLOCK
    qb = q.reshape(B, nb, ATTN_BLOCK, N_KV_HEADS, GROUP, HEAD_DIM).astype(jnp.float32)
    kb = k.reshape(B, nb, ATTN_BLOCK, N_KV_HEADS, HEAD_DIM).astype(jnp.float32)
    vb = v.reshape(B, nb, ATTN_BLOCK, N_KV_HEADS, HEAD_DIM).astype(jnp.float32)
    pad = ((0, 0), (1, 0), (0, 0), (0, 0), (0, 0))
    kk = jnp.concatenate([jnp.pad(kb[:, :-1], pad), kb], axis=2)
    vv = jnp.concatenate([jnp.pad(vb[:, :-1], pad), vb], axis=2)
    s = jnp.einsum('bnqhgd,bnkhd->bnhgqk', qb, kk) * (HEAD_DIM ** -0.5)
    qi = jnp.arange(ATTN_BLOCK)[:, None] + ATTN_BLOCK
    kj = jnp.arange(2 * ATTN_BLOCK)[None, :]
    band = (kj <= qi) & (qi - kj < WINDOW)
    has_prev = (jnp.arange(nb)[:, None, None] > 0) | (kj[None] >= ATTN_BLOCK)
    valid = band[None] & has_prev
    s = jnp.where(valid[None, :, None, None], s, -jnp.inf)
    sink = sinks.astype(jnp.float32).reshape(N_KV_HEADS, GROUP)[None, None, :, :, None, None]
    m = jnp.maximum(jnp.max(s, axis=-1, keepdims=True), sink)
    p = jnp.exp(s - m)
    denom = jnp.sum(p, axis=-1, keepdims=True) + jnp.exp(sink - m)
    o = jnp.einsum('bnhgqk,bnkhd->bnqhgd', p / denom, vv)
    return o.reshape(B, S, ATTN_WIDTH).astype(q.dtype)

def hgrn2_chunkwise(q, k, v, log_f):
    B, S = q.shape[0], q.shape[1]
    nc = S // HGRN_CHUNK

    def to_chunks(t):
        return t.reshape(B, nc, HGRN_CHUNK, HGRN_HEADS, t.shape[-1]).transpose(1, 0, 3, 2, 4)

    causal = jnp.tril(jnp.ones((HGRN_CHUNK, HGRN_CHUNK), dtype=bool))

    def step(state, inp):
        qc, kc, vc, gc = inp
        b = jnp.cumsum(gc, axis=2)
        o_inter = jnp.einsum('bhtk,bhkv->bhtv', qc * jnp.exp(b), state)
        diff = b[:, :, :, None, :] - b[:, :, None, :, :]
        decay = jnp.exp(jnp.where(causal[:, :, None], diff, -jnp.inf))
        a = jnp.einsum('bhtk,bhsk,bhtsk->bhts', qc, kc, decay)
        o_intra = jnp.einsum('bhts,bhsv->bhtv', a, vc)
        b_last = b[:, :, -1:, :]
        state = jnp.exp(b_last[:, :, 0])[..., None] * state + jnp.einsum(
            'bhsk,bhsv->bhkv', kc * jnp.exp(b_last - b), vc)
        return state, o_inter + o_intra

    init = jnp.zeros((B, HGRN_HEADS, HGRN_KEY_DIM, HGRN_VAL_DIM), jnp.float32)
    _, o = lax.scan(step, init, (to_chunks(q), to_chunks(k), to_chunks(v), to_chunks(log_f)))
    return o.transpose(1, 0, 3, 2, 4).reshape(B, S, HGRN_HEADS, HGRN_VAL_DIM)

def hierarchical_moe(xn, w_rg, b_rg, w_re, b_re, w_gate, w_up, w_down):
    T, D = xn.shape
    lg = (xn @ w_rg).astype(jnp.float32) + b_rg.astype(jnp.float32)
    pg = jax.nn.softmax(lg, axis=-1)
    gsel = jnp.argmax(pg, axis=-1)
    pgsel = jnp.take_along_axis(pg, gsel[:, None], axis=1)[:, 0]
    le = ((xn @ w_re).astype(jnp.float32) + b_re.astype(jnp.float32)).reshape(T, N_GROUPS, EXPERTS_PER_GROUP)
    le_sel = jnp.take_along_axis(le, gsel[:, None, None], axis=1)[:, 0]
    pe = jax.nn.softmax(le_sel, axis=-1)
    topv, topi = lax.top_k(pe, TOP_K)
    gate_w = pgsel[:, None] * topv / jnp.sum(topv, axis=-1, keepdims=True)
    eid = gsel[:, None] * EXPERTS_PER_GROUP + topi

    TK = T * TOP_K
    flat_e = eid.reshape(-1).astype(jnp.int32)
    flat_tok = jnp.repeat(jnp.arange(T, dtype=jnp.int32), TOP_K)
    flat_w = gate_w.reshape(-1)
    order = jnp.argsort(flat_e)
    se = flat_e[order]
    counts = jnp.bincount(flat_e, length=N_EXPERTS)
    starts = jnp.cumsum(counts) - counts
    padded = ((counts + MOE_BLOCK - 1) // MOE_BLOCK) * MOE_BLOCK
    pends = jnp.cumsum(padded)
    pstarts = pends - padded
    dest = pstarts[se] + jnp.arange(TK, dtype=jnp.int32) - starts[se]
    P = TK + N_EXPERTS * MOE_BLOCK
    P = ((P + MOE_BLOCK - 1) // MOE_BLOCK) * MOE_BLOCK
    nblk = P // MOE_BLOCK
    row_tok = jnp.full((P,), T, jnp.int32).at[dest].set(flat_tok[order])
    row_w = jnp.zeros((P,), jnp.float32).at[dest].set(flat_w[order])
    blk_e = jnp.minimum(jnp.searchsorted(pends, jnp.arange(nblk, dtype=jnp.int32) * MOE_BLOCK, side='right'),
                        N_EXPERTS - 1)
    x_pad = jnp.concatenate([xn, jnp.zeros((1, D), xn.dtype)], axis=0)
    x_blocks = x_pad[row_tok].reshape(nblk, MOE_BLOCK, D)

    def expert_block(args):
        xb, e = args
        h = jax.nn.silu(xb @ w_gate[e]) * (xb @ w_up[e])
        return h @ w_down[e]

    y_blocks = lax.map(expert_block, (x_blocks, blk_e))
    y_rows = y_blocks.reshape(P, D) * row_w[:, None].astype(y_blocks.dtype)
    return jax.ops.segment_sum(y_rows, row_tok, num_segments=T + 1)[:T]

def second_inputs(seed: int = 0) -> dict:
    key = jax.random.key(seed)
    ks = jax.random.split(key, 24)
    f32 = jnp.float32
    nrm = lambda k, shape, scale: jax.random.normal(k, shape, f32) * scale
    x = jax.random.normal(ks[0], (BATCH, SEQ, D_MODEL), f32)
    offs = jax.random.randint(ks[1], (BATCH, 1), 0, 4096, dtype=jnp.int32)
    positions = offs + jnp.arange(SEQ, dtype=jnp.int32)[None, :]
    return {
        "x": x,
        "positions": positions,
        "norm1_w": 1.0 + nrm(ks[2], (DEPTH_2, D_MODEL), 0.02),
        "w_in": nrm(ks[3], (DEPTH_2, D_MODEL, IN_WIDTH), D_MODEL ** -0.5),
        "q_norm_w": 1.0 + nrm(ks[4], (DEPTH_2, HEAD_DIM), 0.02),
        "k_norm_w": 1.0 + nrm(ks[5], (DEPTH_2, HEAD_DIM), 0.02),
        "attn_sinks": nrm(ks[6], (DEPTH_2, N_Q_HEADS), 0.5),
        "hgrn_lower_bounds": nrm(ks[7], (DEPTH_2 + 1, HGRN_KEY_WIDTH), 0.5),
        "hgrn_norm_w": 1.0 + nrm(ks[8], (DEPTH_2, HGRN_VAL_DIM), 0.02),
        "w_branch_attn": nrm(ks[9], (DEPTH_2, ATTN_WIDTH, D_MODEL), ATTN_WIDTH ** -0.5),
        "w_branch_hgrn": nrm(ks[10], (DEPTH_2, HGRN_WIDTH, D_MODEL), HGRN_WIDTH ** -0.5),
        "w_out": nrm(ks[11], (DEPTH_2, D_MODEL, D_MODEL), D_MODEL ** -0.5),
        "norm2_w": 1.0 + nrm(ks[12], (DEPTH_2, D_MODEL), 0.02),
        "w_router_group": nrm(ks[13], (DEPTH_2, D_MODEL, N_GROUPS), D_MODEL ** -0.5),
        "b_router_group": nrm(ks[14], (DEPTH_2, N_GROUPS), 0.01),
        "w_router_expert": nrm(ks[15], (DEPTH_2, D_MODEL, N_EXPERTS), D_MODEL ** -0.5),
        "b_router_expert": nrm(ks[16], (DEPTH_2, N_EXPERTS), 0.01),
        "w_gate_experts": nrm(ks[17], (DEPTH_2, N_EXPERTS, D_MODEL, EXPERT_FF), D_MODEL ** -0.5),
        "w_up_experts": nrm(ks[18], (DEPTH_2, N_EXPERTS, D_MODEL, EXPERT_FF), D_MODEL ** -0.5),
        "w_down_experts": nrm(ks[19], (DEPTH_2, N_EXPERTS, EXPERT_FF, D_MODEL), EXPERT_FF ** -0.5),
    }

def second_block(x, positions, norm1_w, w_in, q_norm_w, k_norm_w, attn_sinks, hgrn_lower_bounds,
              hgrn_norm_w, w_branch_attn, w_branch_hgrn, w_out, norm2_w, w_router_group,
              b_router_group, w_router_expert, b_router_expert, w_gate_experts, w_up_experts,
              w_down_experts):
    B, S, D = x.shape
    cos, sin = rope_tables(positions)
    split_points = [int(v) for v in np.cumsum(IN_SIZES)[:-1]]
    lower_bounds = jnp.cumsum(jax.nn.softmax(hgrn_lower_bounds.astype(jnp.float32), axis=0), axis=0)
    for l in range(DEPTH_2):
        xn = rms_norm(x, norm1_w[l])
        proj = xn @ w_in[l]
        q_a, k_a, v_a, q_h, f_h, i_h, g_h, z_a, z_b = jnp.split(proj, split_points, axis=-1)

        q_a = partial_rope(rms_norm(q_a.reshape(B, S, N_Q_HEADS, HEAD_DIM), q_norm_w[l]), cos, sin)
        k_a = partial_rope(rms_norm(k_a.reshape(B, S, N_KV_HEADS, HEAD_DIM), k_norm_w[l]), cos, sin)
        v_a = v_a.reshape(B, S, N_KV_HEADS, HEAD_DIM)
        attn = sliding_window_gqa(q_a, k_a, v_a, attn_sinks[l])

        lb = lower_bounds[l]
        fg = lb + (1.0 - lb) * jax.nn.sigmoid(f_h.astype(jnp.float32))
        hq = jax.nn.silu(q_h.astype(jnp.float32)).reshape(B, S, HGRN_HEADS, HGRN_KEY_DIM)
        hk = (1.0 - fg).reshape(B, S, HGRN_HEADS, HGRN_KEY_DIM)
        hlogf = jnp.log(fg).reshape(B, S, HGRN_HEADS, HGRN_KEY_DIM)
        hv = i_h.astype(jnp.float32).reshape(B, S, HGRN_HEADS, HGRN_VAL_DIM)
        ho = rms_norm(hgrn2_chunkwise(hq, hk, hv, hlogf), hgrn_norm_w[l]).reshape(B, S, HGRN_WIDTH)
        hgrn = (ho * jax.nn.silu(g_h.astype(jnp.float32))).astype(x.dtype)

        mixed = (jax.nn.sigmoid(z_a) * (attn @ w_branch_attn[l])
                 + jax.nn.sigmoid(z_b) * (hgrn @ w_branch_hgrn[l]))
        x = x + mixed @ w_out[l]

        hn = rms_norm(x, norm2_w[l]).reshape(B * S, D)
        moe = hierarchical_moe(hn, w_router_group[l], b_router_group[l], w_router_expert[l],
                               b_router_expert[l], w_gate_experts[l], w_up_experts[l], w_down_experts[l])
        x = x + moe.reshape(B, S, D).astype(x.dtype)
    return x


def setup_inputs(seed=0):
    out = dict(first_inputs(seed))
    for name, value in second_inputs(seed + 1).items():
        if name != "x":
            out[name + "_2"] = value
    return out


def reference(
    x, c, ctx, c_ctx, norm_g, ada_w, ada_b, final_g, mla_w_in, mla_q_norm_g, mla_kv_norm_g,
    mla_w_uq, mla_w_ukv, mla_w_out, hy_w_in, hy_conv_w, hy_conv_b, hy_filt_w_in, hy_filt_w_hid,
    hy_filt_b, hy_filt_freq, hy_filt_w_out, hy_bias, hy_w_out, swa_w_in, swa_sink, swa_w_out,
    cf_w_in, cf_dw_w, cf_dw_b, cf_ln_g, cf_ln_b, cf_w_out, positions_2, norm1_w_2, w_in_2,
    q_norm_w_2, k_norm_w_2, attn_sinks_2, hgrn_lower_bounds_2, hgrn_norm_w_2, w_branch_attn_2,
    w_branch_hgrn_2, w_out_2, norm2_w_2, w_router_group_2, b_router_group_2, w_router_expert_2,
    b_router_expert_2, w_gate_experts_2, w_up_experts_2, w_down_experts_2,
):
    x = first_block(
        x, c, ctx, c_ctx, norm_g, ada_w, ada_b, final_g, mla_w_in, mla_q_norm_g, mla_kv_norm_g,
        mla_w_uq, mla_w_ukv, mla_w_out, hy_w_in, hy_conv_w, hy_conv_b, hy_filt_w_in,
        hy_filt_w_hid, hy_filt_b, hy_filt_freq, hy_filt_w_out, hy_bias, hy_w_out, swa_w_in,
        swa_sink, swa_w_out, cf_w_in, cf_dw_w, cf_dw_b, cf_ln_g, cf_ln_b, cf_w_out,
    )
    return second_block(
        x, positions_2, norm1_w_2, w_in_2, q_norm_w_2, k_norm_w_2, attn_sinks_2,
        hgrn_lower_bounds_2, hgrn_norm_w_2, w_branch_attn_2, w_branch_hgrn_2, w_out_2,
        norm2_w_2, w_router_group_2, b_router_group_2, w_router_expert_2, b_router_expert_2,
        w_gate_experts_2, w_up_experts_2, w_down_experts_2,
    )


_drawn_inputs = setup_inputs


def setup_inputs(seed=0):
    import zlib

    import numpy as np

    out = dict(_drawn_inputs(seed))
    spreads = {}
    factors = {'ctx': 3.386,
     'norm_g': 2.979,
     'mla_q_norm_g': 8.0,
     'mla_kv_norm_g': 5.466,
     'hy_filt_freq': 3.332,
     'q_norm_w_2': 5.313,
     'k_norm_w_2': 5.885,
     'attn_sinks_2': 176.655,
     'hgrn_norm_w_2': 9.023,
     'b_router_group_2': 27.948,
     'b_router_expert_2': 10.155,
     'norm2_w_2': 2.871}
    for name, (base, spread) in spreads.items():
        noise = np.random.default_rng([zlib.crc32(name.encode()), seed]).standard_normal(out[name].shape)
        drawn = base * np.exp(spread * noise) if base else spread * noise
        out[name] = __import__('jax').numpy.asarray(drawn.astype(out[name].dtype))
    for name, factor in factors.items():
        out[name] = (out[name] * factor).astype(out[name].dtype)
    return out
```

```python
from contextlib import ExitStack

import numpy as np

import concourse.bass as bass
from concourse import mybir

F32 = mybir.dt.float32
I32 = mybir.dt.int32
U32 = mybir.dt.uint32
U8 = mybir.dt.uint8
ALU = mybir.AluOpType
ACT = mybir.ActivationFunctionType
AX = mybir.AxisListType

P = 128
D = 1024
SEQ = 1024
CTX = 256
KEYS = SEQ + CTX
KT = D // P
TT = SEQ // P
CT = CTX // P
BANK = 512
EPS = 1e-6

Q_RANK, KV_RANK, NOPE, ROPE, VDIM, MLA_HEADS = 384, 256, 128, 64, 128, 8
MLA_SCALE = (NOPE + ROPE) ** -0.5

NFFT = 2 * SEQ
RA, RB = 32, 64
HID = 64
ORDER = 2

HD, QH, KVH, ROT = 64, 8, 2, 16
HG_HEADS = 4
EXPERTS, GROUPS, PER_GROUP, FF = 32, 4, 8, 512
BLOCKS = 2 * SEQ // P + EXPERTS


class Ring:

    def __init__(self, slots, loaded, used):
        self.slots, self.loaded, self.used = slots, loaded, used
        self.chunks, self.sent, self.landed = [], 0, {}
        self.count = [0] * len(slots)

    def plan(self, *parts):
        self.chunks.append(parts)
        return len(self.chunks) - 1

    def send(self, sp, last):
        while self.sent < min(last + 1, len(self.chunks)):
            n = self.sent
            s = n % len(self.slots)
            if n >= len(self.slots):
                sp.wait_ge(self.used, n - len(self.slots) + 1)
            for view, src in self.chunks[n]:
                sp.dma_start(view(self.slots[s]), src).then_inc(self.loaded[s], 16)
                self.count[s] += 16
            self.landed[n] = self.count[s]
            self.sent += 1

    def slot(self, n):
        return self.slots[n % len(self.slots)]

    def landed_at(self, n):
        s = n % len(self.slots)
        at = sum(16 * len(self.chunks[i]) for i in range(s, n + 1, len(self.slots)))
        return self.loaded[s], at


def constants():
    f64, f32 = np.float64, np.float32
    out = {"ident": np.eye(P, dtype=f32)}

    rows = np.repeat(np.arange(SEQ // 64, dtype=f32), 64)
    cols = np.tile(np.arange(64, dtype=f32), SEQ // 64)
    inv = (f32(10000.0) ** (-np.arange(16, dtype=f32) / f32(16))).astype(f32)
    ang = np.concatenate([rows[:, None] * inv, cols[:, None] * inv], -1)
    out["rope_cos"] = np.ascontiguousarray(np.tile(np.cos(ang).astype(f32).T, (4, 1)))
    out["rope_sin"] = np.ascontiguousarray(np.tile(np.sin(ang).astype(f32).T, (4, 1)))
    rot = np.zeros((P, P), f32)
    for h in range(2):
        for i in range(32):
            rot[64 * h + 32 + i, 64 * h + i] = -1.0
            rot[64 * h + i, 64 * h + 32 + i] = 1.0
    out["rope_rot"] = rot

    t = np.linspace(0.0, 1.0, SEQ, dtype=f32)
    wpos = (f32(2.0 * np.pi / SEQ) * np.arange(SEQ, dtype=f32))[:, None]
    bands = np.linspace(1e-4, 15, 16, dtype=f32)[None, :]
    feats = np.concatenate([t[:, None], np.cos(bands * wpos), -np.sin(bands * wpos)], -1).astype(f32)
    lag = np.concatenate([np.arange(SEQ), [0], np.arange(SEQ - 1, 0, -1)])
    out["hy_pos"] = np.ascontiguousarray(feats[lag].T)
    deltas = np.abs(np.linspace(np.log(1e-2) / 0.3, np.log(1e-2) / 1.5, D, dtype=f32))
    out["hy_deltas"] = deltas.reshape(1, D).astype(f32)
    out["hy_negt"] = np.ascontiguousarray(np.stack([-t[lag[g::16]] for g in range(16)], -1).astype(f32))

    theta = f32(500000.0)
    out["swa_inv_freq"] = (theta ** (-np.arange(0, ROT, 2, dtype=f32) / f32(ROT))).astype(f32).reshape(1, -1)
    q, k = np.arange(P)[:, None], np.arange(P)[None, :]
    out["swa_mask"] = np.ascontiguousarray(np.stack([np.where(k > q, 0, -1e30), np.where(k <= q, 0, -1e30)], 1).astype(f32))

    src, dst = np.arange(P)[:, None], np.arange(P)[None, :]
    levels = [src == dst]
    for i in range(7):
        levels.append((src >> i) % 2 == 0)
        levels[-1] = levels[-1] & ((dst >> i) == (src >> i) + 1)
    out["hg_mask"] = np.ascontiguousarray(np.stack(levels, 1).astype(np.int32))

    out["route_iota"] = np.tile(np.arange(P, dtype=f32), (P, 1))
    out["route_tok"] = np.ascontiguousarray(np.arange(SEQ, dtype=f32).reshape(TT, P).T)
    out["route_tri"] = np.triu(np.ones((P, P), f32), 1)

    def first(avals):
        av = np.asarray(avals, f64)
        co = np.zeros((len(av), RA))
        co[:, 0] = 1.0
        co[:, 1] = np.cos(np.pi * av)
        for c in range(1, 16):
            co[:, 2 * c] = np.cos(2 * np.pi * c * av / RA)
            co[:, 2 * c + 1] = -np.sin(2 * np.pi * c * av / RA)
        return co

    one_z = np.zeros((16, 8, RA, 8))
    one_k = np.zeros((RA, 4, RA, 4))
    last = np.zeros((RA, 4, 16, 4))
    cz, ck = first(np.arange(16)), first(np.arange(RA))
    scale = np.full(RA, 2.0)
    scale[0:2] = 1.0
    for i in range(8):
        one_z[:, i, :, i] = cz
    for i in range(4):
        one_k[:, i, :, i] = ck
        last[:, i, :, i] = (cz * scale / NFFT).T
    out["fft_one_z"] = one_z.reshape(P, 8 * RA).astype(f32)
    out["fft_one_k"] = one_k.reshape(P, P).astype(f32)
    out["fft_last"] = last.reshape(P, 64).astype(f32)

    b, d = np.arange(RB), np.arange(RB)
    fwd, back = np.zeros((17, P, 256)), np.zeros((17, P, 192))
    for c in range(17):
        th = 2 * np.pi * np.outer(b, c + RA * d) / NFFT
        co, si = np.cos(th), np.sin(th)
        re, im = np.concatenate([co, si], 0), np.concatenate([-si, co], 0)
        if c == 0:
            re[64:], im[64:] = 0, 0
        if c == 16:
            re, im = np.concatenate([0 * co, co], 0), np.concatenate([0 * co, -si], 0)
        vre, vim = np.concatenate([co.T, -si.T], 0), np.concatenate([si.T, co.T], 0)
        fwd[c] = np.concatenate([re, re, im, im], 1)
        back[c] = np.concatenate([-vim, vre, vim], 1)
    for name, mat in (("fft_fwd", fwd), ("fft_back", back)):
        out[name] = np.ascontiguousarray(mat.transpose(1, 0, 2)).astype(f32)
    return out


class Names:
    pass


class Stage:

    def __init__(self, nc, name):
        self.nc, self.name, self.sems, self.ctx = nc, name, [], ExitStack()

    def __enter__(self):
        return self

    def __exit__(self, *e):
        if e[0] is None:
            self.nc.clear_and_free_semaphores(self.sems)
            self.nc.all_engine_barrier()
        return self.ctx.__exit__(*e)

    def sb(self, name, shape, dt=F32):
        return self.ctx.enter_context(self.nc.sbuf_tensor(f"{self.name}_{name}", shape, dt))

    def ps(self, name, cols=BANK):
        return self.ctx.enter_context(self.nc.psum_tensor(f"{self.name}_{name}", [P, cols], F32))

    def sem(self, name):
        self.sems.append(self.nc.alloc_semaphore(f"{self.name}_{name}"))
        return self.sems[-1]


VEC_A = dict(norm_g0=0, norm_g1=8, final_g=16, c=24, c_ctx=32, ada_b0=40, ada_b1=64)
VEC_B = dict(conv_w=0, conv_b=72)
VEC_C = dict(hy_bias=0, q_norm_g=16, kv_norm_g=19, norm1_w=21, norm2_w=29, hgrn_lb=37, hgrn_norm=45)
VEC_ROWS = (88, 96, 46)


def wait_apart(eng, sem, value, passed):
    eng.wait_ge(sem, value)
    eng.sem_inc(passed, 1)


class RmsNorm:

    STEPS = ("squared", "added", "summed", "variance", "rooted", "inverse", "diagonal", "spread")

    def __init__(self, st, m, width):
        self.m = m
        self.sem = {s: st.sem(f"rms_{s}") for s in self.STEPS}
        self.sq = st.sb("rms_sq", [P, 2, width])
        self.acc = st.sb("rms_acc", [P, width])
        self.small = st.sb("rms_small", [P, 3, width // P])
        self.diag = self.sq[:, 0, :]
        self.stat = st.ps("rms_stat")
        self.rb = st.ps("rms_rb", -(-width // BANK) * BANK)
        self.calls = []

    def plan(self, tiles, tokens, dim):
        base = dict(n=len(self.calls), squared=sum(c[0] for c in self.calls), added=sum(c[0] - 1 for c in self.calls),
                    h=sum(-(-c[1] // BANK) for c in self.calls))
        self.calls.append((tiles, tokens, dim, base))
        return len(self.calls) - 1

    def square(self, act, k, x):
        tiles, tokens, _, base = self.calls[k]
        for f in range(tiles):
            if f == 0:
                dst = self.acc[:, 0:tokens]
                if base["n"]:
                    act.wait_ge(self.sem["summed"], base["n"])
            else:
                slot = base["added"] + f - 1
                dst = self.sq[:, slot % 2, 0:tokens]
                if f == 1 and base["n"]:
                    act.wait_ge(self.sem["spread"], base["h"])
                if slot >= 2:
                    act.wait_ge(self.sem["added"], slot - 1)
            act.activation(dst, x(f), ACT.Square).then_inc(self.sem["squared"], 1)

    def add(self, dve, k):
        tiles, tokens, _, base = self.calls[k]
        for f in range(1, tiles):
            slot = base["added"] + f - 1
            dve.wait_ge(self.sem["squared"], base["squared"] + f + 1)
            if f > 1:
                dve.wait_ge(self.sem["added"], slot)
            dve.tensor_tensor(self.acc[:, 0:tokens], self.acc[:, 0:tokens], self.sq[:, slot % 2, 0:tokens], ALU.add)\
               .then_inc(self.sem["added"], 1)

    def total(self, pe, k):
        tiles, tokens, _, base = self.calls[k]
        if base["n"]:
            pe.wait_ge(self.sem["variance"], base["n"])
        pe.wait_ge(self.sem["squared"], base["squared"] + tiles)
        if tiles > 1:
            pe.wait_ge(self.sem["added"], base["added"] + tiles - 1)
        for t in range(tokens // P):
            mm = pe.matmul(self.stat[:, t:t + 1], self.acc[:, t * P:(t + 1) * P], self.m.ones[:, 0:1], start=True, stop=True)
        mm.then_inc(self.sem["summed"], 1)

    def root(self, act, k):
        tokens, base = self.calls[k][1], self.calls[k][3]
        n = tokens // P
        act.wait_ge(self.sem["variance"], base["n"] + 1)
        act.activation(self.small[:, 1, 0:n], self.small[:, 0, 0:n], ACT.Sqrt).then_inc(self.sem["rooted"], 1)

    def invert(self, dve, k):
        tiles, tokens, dim, base = self.calls[k]
        n = tokens // P
        self.add(dve, k)
        dve.wait_ge(self.sem["summed"], base["n"] + 1)
        dve.tensor_scalar(self.small[:, 0, 0:n], self.stat[:, 0:n], 1.0 / dim, EPS, ALU.mult, ALU.add)\
           .then_inc(self.sem["variance"], 1)
        dve.wait_ge(self.sem["rooted"], base["n"] + 1)
        dve.reciprocal(self.small[:, 2, 0:n], self.small[:, 1, 0:n]).then_inc(self.sem["inverse"], 1)
        dve.wait_ge(self.sem["inverse"], base["n"] + 1)
        if base["h"]:
            dve.wait_ge(self.sem["spread"], base["h"])
        for t in range(n):
            ins = dve.tensor_scalar(self.diag[:, t * P:(t + 1) * P], self.m.ident[:, :], self.small[:, 2, t:t + 1],
                                    None, ALU.mult)
        ins.then_inc(self.sem["diagonal"], 1)

    def spread(self, pe, k):
        tokens, base = self.calls[k][1], self.calls[k][3]
        pe.wait_ge(self.sem["diagonal"], base["n"] + 1)
        for at in range(0, tokens, BANK):
            w = min(BANK, tokens - at)
            pe.matmul(self.rb[:, at:at + w], self.m.ones[:, :], self.diag[:, at:at + w], start=True, stop=True)\
              .then_inc(self.sem["spread"], 1)

    def wait_spread(self, eng, k):
        tokens, base = self.calls[k][1], self.calls[k][3]
        eng.wait_ge(self.sem["spread"], base["h"] + -(-tokens // BANK))


def weight_cols(w, lo, hi):
    return w[:, lo:hi].rearrange("(k p) c -> p k c", p=P)


def slot_cols(n, lo=0, width=None):
    width = n - lo if width is None else width
    return lambda s: s[:, 0:KT * n].rearrange("p (k c) -> p k c", k=KT)[:, :, lo:lo + width]


class Adaptive:

    CHUNKS = 6

    def __init__(self, st, m, layer, banks, out, rows):
        self.m, self.layer, self.chunks, self.banks, self.out = m, layer, m.ada_chunks[layer], banks, out
        self.rows = rows[0:2, 0:2 * BANK].rearrange("p (s c) -> p s c", s=2)
        self.s_row, self.s_col, self.s_bias = st.sem("ada_row"), st.sem("ada_col"), st.sem("ada_bias")

    def product(self, pe, n):
        ring = self.m.ring
        pe.wait_ge(*ring.landed_at(self.chunks[n]))
        if n >= len(self.banks):
            pe.wait_ge(self.s_row, n - len(self.banks) + 1)
        w = ring.slot(self.chunks[n])[:, :].rearrange("p (k c) -> p k c", k=KT)
        for k in range(KT):
            mm = pe.matmul(self.banks[n % len(self.banks)][0:2, :], self.m.cond[:, k, :], w[:, k, :], start=(k == 0), stop=(k == KT - 1))
        mm.then_inc(ring.used, 1)

    def row_out(self, dve, n):
        dve.wait_ge(self.m.ring.used, self.chunks[n] + 1)
        if n >= 2:
            dve.wait_ge(self.s_col, n - 1)
        dve.tensor_copy(self.rows[:, n % 2, :], self.banks[n % len(self.banks)][0:2, :]).then_inc(self.s_row, 1)

    def turn(self, pe, n):
        pe.wait_ge(self.s_row, n + 1)
        for j in range(4):
            at = 2 * (4 * n + j)
            mm = pe.transpose(self.out[:, at:at + 2], self.rows[:, n % 2, j * P:(j + 1) * P], self.m.ident[0:2, 0:2])
        mm.then_inc(self.s_col, 1)

    def columns(self, dve):
        m, layer = self.m, self.layer
        dve.wait_ge(self.s_col, self.CHUNKS)
        at = VEC_A[f"ada_b{layer}"]
        bias = m.vec[0][:, at:at + 24].unsqueeze(2).to_broadcast([P, 24, 2])
        part = self.out[:, 0:48].rearrange("p (c i) -> p c i", i=2)
        dve.tensor_tensor(m.ada[:, layer, :, :], part, bias, ALU.add).then_inc(self.s_bias, 1)
        dve.wait_ge(self.s_bias, 1)
        g = m.vec[0][:, VEC_A[f"norm_g{layer}"]:][:, 0:8]
        for i in range(2):
            dve.scalar_tensor_tensor(out=m.gain[:, layer, i, :], in0=m.ada[:, layer, 8:16, i], scalar=1.0,
                                     in1=g, op0=ALU.add, op1=ALU.mult).then_inc(self.s_bias, 1)
        dve.wait_ge(self.s_bias, 3)


def prepare(nc, m, a, ctx, out):
    ring = m.ring
    m.ada_chunks = [[ring.plan((slot_cols(512), weight_cols(a["ada_w"][layer], 512 * j, 512 * j + 512)))
                     for j in range(Adaptive.CHUNKS)] for layer in range(2)]
    m.chunk_in = [
        ring.plan((slot_cols(512), weight_cols(a["mla_w_in"][0], 0, 512))),
        ring.plan((slot_cols(256, 0, 192), weight_cols(a["mla_w_in"][0], 512, 704)),
                  (slot_cols(256, 192, 64), weight_cols(a["mla_w_in"][0], 640, 704))),
        ring.plan((slot_cols(512), weight_cols(a["mla_w_in"][0], 704, 1216))),
        ring.plan((slot_cols(512), weight_cols(a["mla_w_in"][0], 1216, 1728))),
    ]
    with Stage(nc, "prep") as st:
        xin = st.sb("xin", [P, TT, D])
        cin = st.sb("cin", [P, CT, D])
        rows = [st.sb(f"vec_rows{i}", [P, P]) for i in range(3)]
        vps = st.ps("vec")
        ada = Adaptive(st, m, 0, [st.ps(f"ada{i}") for i in range(2)], vps[:, 3 * P:],
                       st.sb("ada_rows", [2, 2 * BANK]))
        tps = [st.ps(f"turn{i}") for i in range(4)]
        s_const, s_vec, s_x0, s_x1, s_ctx = (st.sem(n) for n in ("const", "vec", "x0", "x1", "ctx"))
        s_ones, s_vturn, s_vcol, s_silu = (st.sem(n) for n in ("ones", "vturn", "vcol", "silu"))
        s_turn, s_even, s_odd = (st.sem(n) for n in ("turn", "even", "odd"))

        groups = []
        for half in range(2):
            for f in range(KT):
                groups.append(([xin[:, 4 * half + t, f * P:(f + 1) * P] for t in range(4)],
                               m.xT[:, f, half * BANK:(half + 1) * BANK]))
        for f in range(0, KT, 2):
            groups.append(([cin[:, t, (f + i) * P:(f + i + 1) * P] for i in range(2) for t in range(CT)],
                           m.ctxT[:, f:f + 2, :]))

        vectors = [
            (0, VEC_A["norm_g0"], a["norm_g"][0], 8), (0, VEC_A["norm_g1"], a["norm_g"][1], 8),
            (0, VEC_A["final_g"], a["final_g"], 8), (0, VEC_A["c"], a["c"][0], 8), (0, VEC_A["c_ctx"], a["c_ctx"], 8),
            (0, VEC_A["ada_b0"], a["ada_b"][0], 24), (0, VEC_A["ada_b1"], a["ada_b"][1], 24),
            (1, VEC_B["conv_w"], a["hy_conv_w"][0].rearrange("k c -> (k c)"), 72),
            (1, VEC_B["conv_b"], a["hy_conv_b"][0], 24),
            (2, VEC_C["hy_bias"], a["hy_bias"][0].rearrange("o c -> (o c)"), 16),
            (2, VEC_C["q_norm_g"], a["mla_q_norm_g"][0], 3), (2, VEC_C["kv_norm_g"], a["mla_kv_norm_g"][0], 2),
            (2, VEC_C["norm1_w"], a["norm1_w_2"][0], 8), (2, VEC_C["norm2_w"], a["norm2_w_2"][0], 8),
            (2, VEC_C["hgrn_lb"], a["hgrn_lower_bounds_2"].rearrange("r c -> (r c)"), 8),
            (2, VEC_C["hgrn_norm"], a["hgrn_norm_w_2"][0], 1),
        ]

        def evacuate(eng, copy, lo, hi, done):
            for g in range(lo, hi, 2):
                eng.wait_ge(s_turn, g + 1)
                dst = groups[g][1]
                src = tps[g % 4][:, :]
                if g >= 2 * KT:
                    src = src.rearrange("p (f t) -> p f t", f=2)
                copy(dst, src).then_inc(done, 1)

        with nc.Block() as block:
            @block.sync
            def _(sp):
                sp.dma_start(m.ident[:, :], a["ident"]).then_inc(s_const, 16)
                xr = a["x"][0].rearrange("(t p) f -> p t f", p=P)
                sp.dma_start(xin[:, 0:4, :], xr[:, 0:4, :]).then_inc(s_x0, 16)
                sp.dma_start(xin[:, 4:8, :], xr[:, 4:8, :]).then_inc(s_x1, 16)
                sp.dma_start(cin[:, :, :], a["ctx"][0].rearrange("(t p) f -> p t f", p=P)).then_inc(s_ctx, 16)
                sp.wait_ge(s_vec, 16 * len(vectors))
                ring.send(sp, ada.chunks[-1] + len(ring.slots))

            @block.scalar
            def _(act):
                for tile, at, src, n in vectors:
                    act.dma_start(rows[tile][at:at + n, :], src.rearrange("(r p) -> r p", p=P)).then_inc(s_vec, 16)
                evacuate(act, lambda o, i: act.activation(o, i, ACT.Copy), 1, KT, s_odd)
                act.wait_ge(s_vcol, 1)
                for i, name in enumerate(("c", "c_ctx")):
                    at = VEC_A[name]
                    act.activation(m.cond[:, :, i], m.vec[0][:, at:at + 8], ACT.Silu).then_inc(s_silu, 1)
                evacuate(act, lambda o, i: act.activation(o, i, ACT.Copy), KT + 1, len(groups), s_odd)

            @block.tensor
            def _(pe):
                pe.wait_ge(s_const, 16)
                for g, (srcs, _) in enumerate(groups):
                    if g == 0:
                        pe.wait_ge(s_x0, 16)
                    if g == KT:
                        pe.wait_ge(s_x1, 16)
                    if g == 2 * KT:
                        pe.wait_ge(s_ctx, 16)
                    if g >= 4:
                        pe.wait_ge(s_odd if g % 2 else s_even, (g - 4) // 2 + 1)
                    for i, src in enumerate(srcs):
                        mm = pe.transpose(tps[g % 4][:, i * P:(i + 1) * P], src, m.ident[:, :])
                    mm.then_inc(s_turn, 1)
                    if g == KT - 1:
                        pe.wait_ge(s_vec, 16 * len(vectors))
                        for i, n in enumerate(VEC_ROWS):
                            pe.transpose(vps[:, i * P:i * P + n], rows[i][0:n, :], m.ident[0:n, 0:n]).then_inc(s_vturn, 1)
                pe.wait_ge(s_silu, 2)
                for n in range(ada.CHUNKS):
                    ada.product(pe, n)
                    if n:
                        ada.turn(pe, n - 1)
                ada.turn(pe, ada.CHUNKS - 1)

            @block.vector
            def _(dve):
                dve.memset(m.ones[:, :], 1.0).then_inc(s_ones, 1)
                evacuate(dve, lambda o, i: dve.tensor_copy(o, i), 0, KT, s_even)
                for i, n in enumerate(VEC_ROWS):
                    dve.wait_ge(s_vturn, 3)
                    dve.tensor_copy(m.vec[i][:, 0:n], vps[:, i * P:i * P + n]).then_inc(s_vcol, 1)
                evacuate(dve, lambda o, i: dve.tensor_copy(o, i), KT, len(groups), s_even)
                for n in range(ada.CHUNKS):
                    ada.row_out(dve, n)
                ada.columns(dve)


def mla_project(nc, m, a):
    ring = m.ring
    chunks = m.chunk_in
    with Stage(nc, "mla_in") as st:
        aT, acT = st.sb("aT", [P, KT, SEQ]), m.ctxT
        norm = RmsNorm(st, m, KEYS)
        tmp = norm.diag
        gemm = [st.ps(f"gemm{i}") for i in range(4)]
        ada = Adaptive(st, m, 1, [b[:, :] for b in gemm[0:3]] + [norm.rb[:, 2 * BANK:3 * BANK]], gemm[3][:, :],
                       m.gateT[:, 0, :])
        n_x, n_c = norm.plan(KT, SEQ, D), norm.plan(KT, CTX, D)
        n_q, n_kv = norm.plan(Q_RANK // P, SEQ, Q_RANK), norm.plan(KV_RANK // P, KEYS, KV_RANK)
        s_tab, s_scaled, s_ready = st.sem("tables"), st.sem("scaled"), st.sem("ready")
        s_mm, s_even, s_odd = st.sem("product"), st.sem("even_out"), st.sem("odd_out")
        s_rot, s_normed, s_roped = st.sem("rotated"), st.sem("normed"), st.sem("roped")

        tiles = []

        def tile(chunk, col, cols, dst, fn=ACT.Copy, with_ctx=False):
            for h in range(2):
                tiles.append((chunk, col, cols, aT[:, :, h * BANK:(h + 1) * BANK], BANK,
                              dst[:, h * BANK:(h + 1) * BANK], fn))
            if with_ctx:
                tiles.append((chunk, col, cols, acT, CTX, dst[:, SEQ:KEYS], fn))

        for j in range(3):
            tile(0, j * P, 512, m.cqT[:, j, :])
        tile(0, 3 * P, 512, m.ckvT[:, 0, :], with_ctx=True)
        tile(1, 0, 256, m.ckvT[:, 1, :], with_ctx=True)
        tile(1, P, 256, m.krT, with_ctx=True)
        for j in range(KT):
            tile(2 + j // 4, (j % 4) * P, 512, m.gateT[:, j, :], ACT.Silu)
        by_act = [i % 2 == 1 or t[6] == ACT.Silu for i, t in enumerate(tiles)]
        done = [(s_odd if x else s_even, sum(1 for y in by_act[:i + 1] if y == x)) for i, x in enumerate(by_act)]
        latents = 15
        assert all(t[6] == ACT.Copy for t in tiles[:latents]) and tiles[latents][6] == ACT.Silu

        def out_of(eng, mine, lo, hi):
            for i in range(lo, hi):
                if by_act[i] != mine:
                    continue
                eng.wait_ge(s_mm, i + 1)
                src, (sem, _) = gemm[i % 4][:, 0:tiles[i][4]], done[i]
                if mine:
                    eng.activation(tiles[i][5], src, tiles[i][6]).then_inc(sem, 1)
                else:
                    eng.tensor_copy(tiles[i][5], src).then_inc(sem, 1)

        def wait_latents(eng, sides):
            for x in sides:
                last = max(i for i in range(latents) if by_act[i] == x)
                eng.wait_ge(*done[last])

        with nc.Block() as block:
            @block.sync
            def _(sp):
                sp.dma_start(m.cos[:, :], a["rope_cos"]).then_inc(s_tab, 16)
                sp.dma_start(m.sin[:, :], a["rope_sin"]).then_inc(s_tab, 16)
                sp.dma_start(m.rot[:, :], a["rope_rot"]).then_inc(s_tab, 16)
                ring.send(sp, chunks[-1])

            @block.scalar
            def _(act):
                norm.square(act, n_x, lambda f: m.xT[:, f, :])
                norm.root(act, n_x)
                norm.square(act, n_c, lambda f: m.ctxT[:, f, :])
                norm.root(act, n_c)
                for i, dst in enumerate((aT, acT)):
                    for f in range(KT):
                        act.wait_ge(s_scaled, i * KT + f + 1)
                        act.activation(dst[:, f, :], dst[:, f, :], ACT.Identity, bias=m.ada[:, 0, f, i:i + 1])\
                           .then_inc(s_ready, 1)
                out_of(act, True, 0, latents)
                wait_latents(act, (False,))
                norm.square(act, n_q, lambda f: m.cqT[:, f, :])
                norm.root(act, n_q)
                norm.square(act, n_kv, lambda f: m.ckvT[:, f, :])
                norm.root(act, n_kv)
                out_of(act, True, latents, len(tiles))

            @block.tensor
            def _(pe):
                norm.total(pe, n_x)
                ada.product(pe, 0)
                norm.spread(pe, n_x)
                ada.product(pe, 1)
                norm.total(pe, n_c)
                ada.product(pe, 2)
                pe.wait_ge(s_scaled, KT)
                norm.spread(pe, n_c)
                ada.product(pe, 3)
                for n in range(4, ada.CHUNKS):
                    ada.turn(pe, n - 4)
                    ada.product(pe, n)
                for n in range(2, ada.CHUNKS):
                    ada.turn(pe, n)
                pe.wait_ge(ada.s_bias, 1)

                def product(lo, hi):
                    for i in range(lo, hi):
                        chunk, col, cols, src, n, _, _ = tiles[i]
                        if i == 0 or tiles[i - 1][0] != chunk:
                            pe.wait_ge(*ring.landed_at(chunks[chunk]))
                        if i >= 4:
                            pe.wait_ge(*done[i - 4])
                        w = ring.slot(chunks[chunk])[:, 0:KT * cols].rearrange("p (k c) -> p k c", k=KT)
                        if i == 0:
                            pe.wait_ge(s_ready, KT)
                        if n == CTX:
                            pe.wait_ge(s_ready, 2 * KT)
                        for k in range(KT):
                            mm = pe.matmul(gemm[i % 4][:, 0:n], w[:, k, col:col + P], src[:, k, :],
                                           start=(k == 0), stop=(k == KT - 1))
                        mm.then_inc(s_mm, 1)
                        if i + 1 == len(tiles) or tiles[i + 1][0] != chunk:
                            pe.wait_ge(s_mm, i + 1)
                            pe.sem_inc(ring.used, 1)

                product(0, latents)
                norm.total(pe, n_q)
                norm.spread(pe, n_q)
                norm.total(pe, n_kv)
                pe.wait_ge(s_normed, Q_RANK // P)
                norm.spread(pe, n_kv)
                pe.wait_ge(s_tab, 48)
                wait_latents(pe, (True, False))
                for h in range(2):
                    pe.matmul(gemm[(latents + h) % 4][:, :], m.rot[:, :], m.krT[:, h * BANK:(h + 1) * BANK],
                              start=True, stop=True).then_inc(s_rot, 1)
                pe.wait_ge(s_roped, 6)
                product(latents, len(tiles))

            @block.vector
            def _(dve):
                for i, (k, src, dst, n) in enumerate(((n_x, m.xT, aT, SEQ), (n_c, m.ctxT, acT, CTX))):
                    norm.invert(dve, k)
                    norm.wait_spread(dve, k)
                    for f in range(KT):
                        dve.scalar_tensor_tensor(out=dst[:, f, :], in0=src[:, f, :], scalar=m.gain[:, 0, i, f:f + 1],
                                                 in1=norm.rb[:, 0:n], op0=ALU.mult, op1=ALU.mult).then_inc(s_scaled, 1)
                for n in range(ada.CHUNKS):
                    ada.row_out(dve, n)
                ada.columns(dve)
                out_of(dve, False, 0, latents)
                for k, name, dst in ((n_q, "q_norm_g", m.cqT), (n_kv, "kv_norm_g", m.ckvT)):
                    norm.invert(dve, k)
                    norm.wait_spread(dve, k)
                    for f in range(dst.shape[1]):
                        at = VEC_C[name] + f
                        dve.scalar_tensor_tensor(out=dst[:, f, :], in0=dst[:, f, :], scalar=m.vec[2][:, at:at + 1],
                                                 in1=norm.rb[:, 0:dst.shape[2]], op0=ALU.mult, op1=ALU.mult)\
                           .then_inc(s_normed, 1)
                dve.wait_ge(s_tab, 48)
                for h in range(2):
                    cols = slice(h * BANK, (h + 1) * BANK)
                    dve.wait_ge(s_rot, 2)
                    dve.tensor_tensor(tmp[:, cols], gemm[(latents + h) % 4][:, :], m.sin[:, cols], ALU.mult)\
                       .then_inc(s_roped, 1)
                    dve.tensor_tensor(m.krT[:, cols], m.krT[:, cols], m.cos[:, cols], ALU.mult).then_inc(s_roped, 1)
                    dve.wait_ge(s_roped, 3 * h + 2)
                    dve.tensor_tensor(m.krT[:, cols], m.krT[:, cols], tmp[:, cols], ALU.add).then_inc(s_roped, 1)
                out_of(dve, False, latents, len(tiles))


def mla_attend(nc, m, a, spare):
    ring = m.ring
    PAIRS, TILES, KB = MLA_HEADS // 2, 2 * TT, KEYS // P
    QB, UP = 2 * (NOPE + ROPE), 2 * (NOPE + VDIM)
    with Stage(nc, "mla") as st:
        wq, wkv = st.sb("wq", [P, Q_RANK // P, QB]), st.sb("wkv", [P, KV_RANK // P, UP])
        qn, qr = st.sb("qn", [P, 2, SEQ]), st.sb("qr", [P, SEQ])
        kn, v = st.sb("kn", [P, 2, KEYS]), st.sb("v", [P, KB, 2 * VDIM])
        prob = st.sb("prob", [P, 2, KEYS])
        tmp = prob[:, :, 0:BANK]
        probT = ring.slot(spare)[:, 0:2 * KEYS].rearrange("p (s b q) -> p s b q", s=2, q=P)
        diag = st.sb("diag", [P, 2, P])
        top, low, tot, inv = (st.sb(n, [P, 2]) for n in ("top", "low", "tot", "inv"))
        gated = st.sb("gated", [P, 2, P])
        SLOT, OUT = 3 * BANK, KEYS
        sc = st.ps("scores", 2 * SLOT)
        tp = [st.ps(f"turn{i}") for i in range(2)]
        s_w, s_proj, s_pa, s_pv = st.sem("weights"), st.sem("projected"), st.sem("by_act"), st.sem("by_dve")
        s_rot, s_rope, s_score, s_top, s_low = (st.sem(n) for n in ("rotated", "roped", "score", "top", "low"))
        s_exp, s_inv, s_diag, s_turn, s_ta, s_tv = (st.sem(n) for n in ("exp", "inv", "diag", "turned", "turn_act", "turn_dve"))
        s_o, s_gate, s_head = st.sem("o"), st.sem("gated"), st.sem("head")
        assert KV_RANK // P == 2

        proj = []
        for c in range(2):
            cols = slice(c * BANK, (c + 1) * BANK)
            proj.append(([(wq[:, k, 2 * NOPE:QB], m.cqT[:, k, cols]) for k in range(3)], BANK, qr[:, cols]))
        for h in range(2):
            for c in range(2):
                cols = slice(c * BANK, (c + 1) * BANK)
                proj.append(([(wq[:, k, h * NOPE:(h + 1) * NOPE], m.cqT[:, k, cols]) for k in range(3)], BANK,
                             qn[:, h, cols]))
        for h in range(2):
            for at, n in ((0, 512), (512, 512), (1024, 256)):
                proj.append(([(wkv[:, k, 256 * h:256 * h + NOPE], m.ckvT[:, k, at:at + n]) for k in range(2)], n,
                             kn[:, h, at:at + n]))
        vals = [wkv[:, k, :].rearrange("p (h c) -> p h c", h=2)[:, :, NOPE:] for k in range(2)]
        for b in range(KB):
            proj.append(([(m.ckvT[:, k, b * P:(b + 1) * P], vals[k]) for k in range(2)], 2 * VDIM, v[:, b, :]))
        NPROJ = len(proj)
        BANKS = 6
        A_N = sum(1 for i in range(NPROJ) if i % 2)
        V_N = NPROJ - A_N

        def copied(i):
            return (s_pa, i // 2 + 1, A_N) if i % 2 else (s_pv, i // 2 + 1, V_N)

        def bank(i):
            return sc[:, (i % BANKS) * BANK:(i % BANKS) * BANK + proj[i][1]]

        with nc.Block() as block:
            @block.sync
            def _(sp):
                m.prefetch(sp)
                with sp.Fori(0, PAIRS) as hp:
                    sp.wait_ge(s_pa, hp * A_N)
                    sp.wait_ge(s_pv, hp * V_N)
                    uq = a["mla_w_uq"][0].rearrange("(k p) c -> p k c", p=P)
                    for h in range(2):
                        at = hp * QB + h * (NOPE + ROPE)
                        sp.dma_start(wq[:, :, h * NOPE:(h + 1) * NOPE], uq[:, :, bass.ds(at, NOPE)]).then_inc(s_w, 16)
                        sp.dma_start(wq[:, :, 2 * NOPE + h * ROPE:2 * NOPE + (h + 1) * ROPE],
                                     uq[:, :, bass.ds(at + NOPE, ROPE)]).then_inc(s_w, 16)
                    sp.dma_start(wkv[:, :, :], a["mla_w_ukv"][0].rearrange("(k p) c -> p k c", p=P)[:, :, bass.ds(hp * UP, UP)])\
                      .then_inc(s_w, 16)

            @block.scalar
            def _(act):
                with act.Fori(0, PAIRS) as hp:
                    for i in range(1, NPROJ, 2):
                        act.wait_ge(s_proj, hp * NPROJ + i + 1)
                        act.activation(proj[i][2], bank(i), ACT.Copy).then_inc(s_pa, 1)

                    def turned(i):
                        act.wait_ge(s_turn, hp * 3 * TILES + 3 * i + 2)
                        act.activation(probT[:, i % 2, 4:8, :], tp[(3 * i + 1) % 2][:, :].rearrange("p (b q) -> p b q", q=P),
                                       ACT.Copy).then_inc(s_ta, 1)

                    for i in range(TILES):
                        act.wait_ge(s_low, hp * TILES + i + 1)
                        if i >= 2:
                            act.wait_ge(s_turn, hp * 3 * TILES + 3 * (i - 1))
                        lo = SLOT * (i % 2)
                        act.activation(prob[:, i % 2, :], sc[:, lo:lo + KEYS], ACT.Exp, bias=low[:, i % 2:i % 2 + 1],
                                       scale=MLA_SCALE, accum_out=tot[:, i % 2:i % 2 + 1]).then_inc(s_exp, 1)
                        turned(i)

            @block.vector
            def _(dve):
                with dve.Fori(0, PAIRS) as hp:
                    for i in range(0, 8, 2):
                        dve.wait_ge(s_proj, hp * NPROJ + i + 1)
                        dve.tensor_copy(proj[i][2], bank(i)).then_inc(s_pv, 1)
                    for c in range(2):
                        cols = slice(c * BANK, (c + 1) * BANK)
                        dve.wait_ge(s_rot, 2 * hp + c + 1)
                        dve.tensor_tensor(tmp[:, c, :], tp[c][:, :], m.sin[:, cols], ALU.mult).then_inc(s_rope, 1)
                        dve.tensor_tensor(qr[:, cols], qr[:, cols], m.cos[:, cols], ALU.mult).then_inc(s_rope, 1)
                        dve.wait_ge(s_rope, 6 * hp + 3 * c + 2)
                        dve.tensor_tensor(qr[:, cols], qr[:, cols], tmp[:, c, :], ALU.add).then_inc(s_rope, 1)
                    for i in range(8, NPROJ, 2):
                        dve.wait_ge(s_proj, hp * NPROJ + i + 1)
                        dve.tensor_copy(proj[i][2], bank(i)).then_inc(s_pv, 1)

                    def maximum(i):
                        s = i % 2
                        lo = SLOT * s
                        dve.wait_ge(s_score, hp * TILES + i + 1)
                        dve.tensor_reduce(top[:, s:s + 1], sc[:, lo:lo + KEYS], AX.X, ALU.max).then_inc(s_top, 1)
                        dve.wait_ge(s_top, hp * TILES + i + 1)
                        if i >= 2:
                            dve.wait_ge(s_exp, hp * TILES + i - 1)
                        dve.tensor_scalar(low[:, s:s + 1], top[:, s:s + 1], -MLA_SCALE, None, ALU.mult).then_inc(s_low, 1)

                    def inverse(i):
                        s = i % 2
                        dve.wait_ge(s_exp, hp * TILES + i + 1)
                        dve.reciprocal(inv[:, s:s + 1], tot[:, s:s + 1]).then_inc(s_inv, 1)
                        dve.wait_ge(s_inv, hp * TILES + i + 1)
                        dve.tensor_scalar(diag[:, s, :], m.ident[:, :], inv[:, s:s + 1], None, ALU.mult).then_inc(s_diag, 1)

                    def turned_out(i, part, b, n):
                        dve.wait_ge(s_turn, hp * 3 * TILES + 3 * i + part + 1)
                        dve.tensor_copy(probT[:, i % 2, b:b + n, :],
                                        tp[(3 * i + part) % 2][:, 0:n * P].rearrange("p (b q) -> p b q", q=P)).then_inc(s_tv, 1)

                    def gate(i):
                        s, head, q = i % 2, 2 * hp + i // TT, (i % TT) * P
                        dve.wait_ge(s_o, hp * TILES + i + 1)
                        lo = SLOT * (1 - s) + OUT
                        dve.tensor_tensor(gated[:, s, :], sc[:, lo:lo + P],
                                          m.gateT[:, bass.ds(head, 1), q:q + P].rearrange("p o q -> p (o q)"), ALU.mult)\
                           .then_inc(s_gate, 1)
                        dve.wait_ge(s_gate, hp * TILES + i + 1)
                        dve.tensor_tensor(m.gateT[:, bass.ds(head, 1), q:q + P].rearrange("p o q -> p (o q)"),
                                          gated[:, s, :], sc[:, lo + P:lo + 2 * P], ALU.mult).then_inc(s_head, 1)

                    maximum(0)
                    for i in range(TILES):
                        turned_out(i, 0, 0, 4)
                        if i + 1 < TILES:
                            maximum(i + 1)
                        inverse(i)
                        if i >= 1:
                            gate(i - 1)
                        turned_out(i, 2, 8, 2)
                    gate(TILES - 1)

            @block.tensor
            def _(pe):
                with pe.Fori(0, PAIRS) as hp:
                    pe.wait_ge(s_w, 80 * (hp + 1))
                    pe.wait_ge(s_head, hp * TILES)
                    for i, (pairs, n, _) in enumerate(proj):
                        if i == 6:
                            pe.wait_ge(s_pv, hp * V_N + 1)
                            pe.wait_ge(s_pa, hp * A_N + 1)
                            for c in range(2):
                                pe.matmul(tp[c][:, :], m.rot[:, :], qr[:, c * BANK:(c + 1) * BANK],
                                          start=True, stop=True).then_inc(s_rot, 1)
                        if i >= BANKS:
                            sem, at, turn = copied(i - BANKS)
                            pe.wait_ge(sem, hp * turn + at)
                        for k, (left, right) in enumerate(pairs):
                            mm = pe.matmul(bank(i), left, right, start=(k == 0), stop=(k == len(pairs) - 1))
                        mm.then_inc(s_proj, 1)
                    pe.wait_ge(s_pa, (hp + 1) * A_N)
                    pe.wait_ge(s_pv, (hp + 1) * V_N)
                    pe.wait_ge(s_rope, 6 * (hp + 1))

                    def scores(i):
                        h, q = i // TT, (i % TT) * P
                        if i >= 2:
                            pe.wait_ge(s_exp, hp * TILES + i - 1)
                        for at in range(0, KEYS, BANK):
                            n, col = min(BANK, KEYS - at), SLOT * (i % 2) + at
                            if n < BANK and i >= 3:
                                pe.wait_ge(s_head, hp * TILES + i - 2)
                            pe.matmul(sc[:, col:col + n], qn[:, h, q:q + P], kn[:, h, at:at + n], start=True, stop=False)
                            mm = pe.matmul(sc[:, col:col + n], qr[64 * h:64 * h + 64, q:q + P],
                                           m.krT[64 * h:64 * h + 64, at:at + n], start=False, stop=True)
                        mm.then_inc(s_score, 1)

                    def turn(i, parts):
                        pe.wait_ge(s_exp, hp * TILES + i + 1)
                        for part in parts:
                            b, n = ((0, 4), (4, 4), (8, 2))[part]
                            if part == 2:
                                pe.wait_ge(s_tv, hp * 2 * TILES + 2 * i + 1)
                            elif i >= 1 and part == 0:
                                pe.wait_ge(s_ta, hp * TILES + i)
                            elif i >= 1:
                                pe.wait_ge(s_tv, hp * 2 * TILES + 2 * i)
                            for j in range(n):
                                mm = pe.transpose(tp[(3 * i + part) % 2][:, j * P:(j + 1) * P],
                                                  prob[:, i % 2, (b + j) * P:(b + j + 1) * P], m.ident[:, :])
                            mm.then_inc(s_turn, 1)

                    def values(i):
                        h, s, lo = i // TT, i % 2, SLOT * (1 - i % 2) + OUT
                        pe.wait_ge(s_tv, hp * 2 * TILES + 2 * i + 2)
                        pe.wait_ge(s_ta, hp * TILES + i + 1)
                        for b in range(KB):
                            pe.matmul(sc[:, lo:lo + P], v[:, b, h * VDIM:(h + 1) * VDIM], probT[:, s, b, :],
                                      start=(b == 0), stop=(b == KB - 1))
                        pe.wait_ge(s_diag, hp * TILES + i + 1)
                        pe.matmul(sc[:, lo + P:lo + 2 * P], m.ones[:, :], diag[:, s, :], start=True, stop=True)\
                          .then_inc(s_o, 1)

                    scores(0)
                    for i in range(TILES):
                        if i + 1 < TILES:
                            scores(i + 1)
                        turn(i, (0, 1))
                        if i >= 1:
                            values(i - 1)
                        turn(i, (2,))
                    values(TILES - 1)


def add_product(nc, m, chunks, src, name, gate=None, spill=None):
    ring = m.ring
    with Stage(nc, name) as st:
        gemm = [st.ps(f"gemm{i}") for i in range(8)]
        s_mm, s_add, s_src = st.sem("product"), st.sem("added"), st.sem("source")
        with nc.Block() as block:
            @block.sync
            def _(sp):
                if spill is not None:
                    sp.dma_start(src[:, :, :], spill.rearrange("f p t -> p f t")).then_inc(s_src, 16)
                m.prefetch(sp)

            @block.tensor
            def _(pe):
                if spill is not None:
                    pe.wait_ge(s_src, 16)
                for i in range(2 * KT):
                    f, h = i // 2, i % 2
                    chunk = chunks[f // 4]
                    if i % 8 == 0:
                        pe.wait_ge(*ring.landed_at(chunk))
                    if i >= 8:
                        pe.wait_ge(s_add, i - 7)
                    w = ring.slot(chunk)[:, :].rearrange("p (k c) -> p k c", k=KT)
                    for k in range(KT):
                        mm = pe.matmul(gemm[i % 8][:, :], w[:, k, (f % 4) * P:(f % 4 + 1) * P],
                                       src[:, k, h * BANK:(h + 1) * BANK], start=(k == 0), stop=(k == KT - 1))
                    mm.then_inc(s_mm, 1)
                    if i % 8 == 7:
                        pe.wait_ge(s_mm, i + 1)
                        pe.sem_inc(ring.used, 1)

            @block.vector
            def _(dve):
                for i in range(2 * KT):
                    f, cols = i // 2, slice((i % 2) * BANK, (i % 2 + 1) * BANK)
                    dve.wait_ge(s_mm, i + 1)
                    if gate is None:
                        dve.tensor_tensor(m.xT[:, f, cols], gemm[i % 8][:, :], m.xT[:, f, cols], ALU.add).then_inc(s_add, 1)
                    else:
                        dve.scalar_tensor_tensor(out=m.xT[:, f, cols], in0=gemm[i % 8][:, :], scalar=gate(f),
                                                 in1=m.xT[:, f, cols], op0=ALU.mult, op1=ALU.add).then_inc(s_add, 1)


def mla_layer(nc, m, a, ctx, out):
    with ExitStack() as c:
        def sb(name, shape):
            return c.enter_context(nc.sbuf_tensor(name, shape, F32))

        m.gateT = sb("gateT", [P, KT, SEQ])
        m.cqT, m.ckvT, m.krT = sb("cqT", [P, 3, SEQ]), sb("ckvT", [P, 2, KEYS]), sb("krT", [P, KEYS])
        m.cos, m.sin, m.rot = sb("cos", [P, SEQ]), sb("sin", [P, SEQ]), sb("rot", [P, P])
        with ExitStack() as c2:
            m.ctxT = c2.enter_context(nc.sbuf_tensor("ctxT", [P, KT, CTX], F32))
            prepare(nc, m, a, ctx, out)
            mla_project(nc, m, a)
        o_chunks = [m.ring.plan((slot_cols(512), weight_cols(a["mla_w_out"][0], 512 * j, 512 * j + 512))) for j in range(2)]
        m.prefetch = lambda sp: m.ring.send(sp, o_chunks[-1])
        mla_attend(nc, m, a, o_chunks[-1] + 1)
        add_product(nc, m, o_chunks, m.gateT, "mla_out", lambda f: m.ada[:, 0, 16 + f, 0:1])


def hyena_prepare(nc, m, a):
    COLS, CH = NFFT, NFFT // BANK
    TWO_PI_HI, MAGIC = 6.28125, 1.5 * 2.0 ** 23
    TWO_PI_LO = 2.0 * np.pi - TWO_PI_HI
    PI_DOWN = 3.1415925
    with Stage(nc, "hy_in") as st:
        norm = RmsNorm(st, m, SEQ)
        n_x = norm.plan(KT, SEQ, D)
        pos = st.sb("pos", [33, COLS])
        w0, wh = st.sb("w0", [33, P]), st.sb("wh", [HID, 2, P])
        par_rows, par = st.sb("par_rows", [6, P]), st.sb("par", [P, 6])
        arg, turn, hid = st.sb("arg", [P, COLS]), st.sb("turn", [P, COLS]), st.sb("hid", [P, COLS])
        pre = st.ps("pre", COLS)
        s_in, s_spill, s_scaled, s_ready = st.sem("in"), st.sem("spill"), st.sem("scaled"), st.sem("ready")
        s_mm, s_arg, s_red, s_sin, s_zero, s_par = (st.sem(n) for n in ("product", "arg", "reduced", "sine", "zero", "par"))
        RED = 5
        with nc.Block() as block:
            @block.sync
            def _(sp):
                sp.dma_start(pos[:, :], a["hy_pos"]).then_inc(s_in, 16)
                for c in range(2):
                    cols = slice(c * HID, (c + 1) * HID)
                    sp.dma_start(w0[:, cols], a["hy_filt_w_in"][0]).then_inc(s_in, 16)
                    sp.dma_start(wh[:, :, cols], a["hy_filt_w_hid"][0].rearrange("l i o -> i l o")).then_inc(s_in, 16)
                    sp.dma_start(par_rows[0:3, cols], a["hy_filt_b"][0]).then_inc(s_in, 16)
                    sp.dma_start(par_rows[3:6, cols], a["hy_filt_freq"][0]).then_inc(s_in, 16)
                sp.dma_start(m.x_spill.rearrange("f p t -> p f t"), m.xT[:, :, :]).then_inc(s_spill, 16)
                sp.wait_ge(s_spill, 16)

            @block.scalar
            def _(act):
                norm.square(act, n_x, lambda f: m.xT[:, f, :])
                norm.root(act, n_x)
                for f in range(KT):
                    act.wait_ge(s_scaled, f + 1)
                    act.activation(m.aT[:, f, :], m.aT[:, f, :], ACT.Identity, bias=m.ada[:, 1, f, 0:1]).then_inc(s_ready, 1)
                for layer in range(3):
                    act.wait_ge(s_red, RED * (layer + 1))
                    if layer < 2:
                        act.activation(hid[:, :], arg[:, :], ACT.Sin).then_inc(s_sin, 1)
                        continue
                    act.wait_ge(s_zero, 1)
                    for rows, lo, hi in ((0, 0, SEQ), (HID, SEQ + 1, NFFT), (HID, 0, 1)):
                        act.activation(m.lags[rows:rows + HID, lo:hi], arg[rows:rows + HID, lo:hi], ACT.Sin)\
                           .then_inc(s_sin, 1)

            @block.tensor
            def _(pe):
                norm.total(pe, n_x)
                norm.spread(pe, n_x)
                pe.wait_ge(s_in, 16 * 9)
                pe.transpose(pre[:, 0:6], par_rows[:, :], m.ident[0:6, 0:6]).then_inc(s_par, 1)
                pe.wait_ge(s_par, 2)
                for layer in range(3):
                    if layer:
                        pe.wait_ge(s_sin, layer)
                    for j in range(CH):
                        cols = slice(j * BANK, (j + 1) * BANK)
                        mm = pe.matmul(pre[:, cols], w0[:, :] if layer == 0 else wh[:, layer - 1, :],
                                       pos[:, cols] if layer == 0 else hid[0:HID, cols], start=True, stop=True)
                    mm.then_inc(s_mm, 1)

            @block.vector
            def _(dve):
                dve.memset(m.lags[:, :], 0.0).then_inc(s_zero, 1)
                norm.invert(dve, n_x)
                norm.wait_spread(dve, n_x)
                for f in range(KT):
                    dve.scalar_tensor_tensor(out=m.aT[:, f, :], in0=m.xT[:, f, :], scalar=m.gain[:, 1, 0, f:f + 1],
                                             in1=norm.rb[:, 0:SEQ], op0=ALU.mult, op1=ALU.mult).then_inc(s_scaled, 1)
                dve.wait_ge(s_par, 1)
                dve.tensor_copy(par[:, :], pre[:, 0:6]).then_inc(s_par, 1)
                dve.wait_ge(s_par, 2)
                for layer in range(3):
                    dve.wait_ge(s_mm, layer + 1)
                    dve.tensor_scalar(arg[:, :], pre[:, :], par[:, layer:layer + 1], par[:, 3 + layer:4 + layer],
                                      ALU.add, ALU.mult).then_inc(s_arg, 1)
                    dve.wait_ge(s_arg, layer + 1)
                    dve.tensor_scalar(turn[:, :], arg[:, :], 1.0 / (2.0 * np.pi), MAGIC, ALU.mult, ALU.add).then_inc(s_red, 1)
                    dve.wait_ge(s_red, RED * layer + 1)
                    dve.tensor_scalar(turn[:, :], turn[:, :], MAGIC, None, ALU.subtract).then_inc(s_red, 1)
                    for i, part in enumerate((TWO_PI_HI, TWO_PI_LO)):
                        dve.wait_ge(s_red, RED * layer + 2 + i)
                        dve.scalar_tensor_tensor(out=arg[:, :], in0=turn[:, :], scalar=-part, in1=arg[:, :],
                                                 op0=ALU.mult, op1=ALU.add).then_inc(s_red, 1)
                    dve.wait_ge(s_red, RED * layer + 4)
                    dve.tensor_scalar(arg[:, :], arg[:, :], PI_DOWN, -PI_DOWN, ALU.min, ALU.max).then_inc(s_red, 1)


class Schedule:

    JOBS = dict(K=4, S1f=4, Tf=4, S2f=9, Tz=2, S1z=4, T2z=4, S2z=5, S3=4, Tv=4, S4=2)
    VECTOR_ONLY = ("K", "S2z", "S4")

    def __init__(self, steps):
        self.jobs, self.first = [], {}
        for step in steps:
            if step[0] == "U":
                continue
            self.first[step] = len(self.jobs)
            for k in range(self.JOBS[step[0]]):
                self.jobs.append((step, k, step[0] not in self.VECTOR_ONLY and k % 2 == 0))
        self.act_turn = sum(j[2] for j in self.jobs)
        self.dve_turn = len(self.jobs) - self.act_turn

    def copied(self, n):
        act = sum(j[2] for j in self.jobs[:n])
        return act, n - act

    def after(self, step):
        return self.copied(self.first[step] + self.JOBS[step[0]])


def hyena_convolve(nc, m, a):
    U_STEPS = 4
    steps = [("U", 0), ("U", 1), ("K", 0), ("U", 2), ("S1f", 0), ("Tz", 0), ("Tf", 0), ("S1z", 0), ("S2f", 0), ("T2z", 0),
             ("K", 1), ("S2z", 0), ("U", 3), ("S3", 0), ("S1f", 1), ("Tv", 0), ("Tf", 1), ("S4", 0), ("S2f", 1), ("U", 4),
             ("Tz", 1), ("U", 5), ("S1z", 1), ("T2z", 1), ("S2z", 1), ("U", 6), ("S3", 1), ("U", 7), ("Tv", 1), ("S4", 1)]
    sched = Schedule(steps)
    NJ = len(sched.jobs)
    ring = m.ring
    with Stage(nc, "hyena") as st:
        w_in = ring.slots[0][:, :].rearrange("p (k j c) -> p k j c", k=KT, j=U_STEPS)
        eF, tF = ring.slots[1][:, 0:2048], ring.slots[1][:, 2048:4096].rearrange("p (s c) -> p s c", c=P)
        eZ, tZ = ring.slots[2][:, 0:2048], ring.slots[2][:, 2048:4096].rearrange("p (s c) -> p s c", c=P)
        room = m.xT[:, :, :].rearrange("p f t -> p (f t)")
        p1 = room[:, 0:2176].rearrange("p (c h) -> p c h", h=P)
        p2 = room[:, 2176:4352].rearrange("p (c h) -> p c h", h=P)
        decay = room[:, 4352:6400].rearrange("p (g h) -> p g h", h=P)
        zt = room[:, 6400:7424].rearrange("p (g h) -> p g h", h=P)
        spec = st.sb("spec", [P, 17, 2, P])
        kt = st.sb("kt", [P, 16, P])
        one_z, one_k, last = st.sb("one_z", [P, 256]), st.sb("one_k", [P, P]), st.sb("last", [P, 64])
        fwd, back = st.sb("fwd", [P, 17, 256]), st.sb("back", [P, 17, 192])
        negt, deltas, w_lag = st.sb("negt", [P, 16]), st.sb("deltas", [P, P]), st.sb("w_lag", [P, ORDER, P])
        conv, gate = st.sb("conv", [P, 3, SEQ]), st.sb("gate", [P, SEQ])
        zout, mix = st.sb("zout", [P, SEQ]), st.sb("mix", [P, SEQ])
        up = [st.ps(f"up{i}", SEQ) for i in range(2)]
        bank = [st.ps(f"bank{i}") for i in range(4)]
        s_tab, s_w, s_lagw, s_delta = st.sem("tables"), st.sem("weights"), st.sem("lag_weights"), st.sem("deltas")
        s_store, s_up, s_mid, s_conv, s_gate = (st.sem(n) for n in ("stored", "up", "middle", "conv", "gate"))
        s_exp_in, s_decay, s_job, s_act, s_dve = (st.sem(n) for n in ("exponent", "decay", "job", "act_out", "dve_out"))
        s_mix, s_z, s_apart, s_back = st.sem("mix"), st.sem("z"), st.sem("apart"), st.sem("back")
        TABS = 6

        def wait_copied(eng, ct, counts):
            if counts[0]:
                eng.wait_ge(s_act, ct * sched.act_turn + counts[0])
            if counts[1]:
                eng.wait_ge(s_dve, ct * sched.dve_turn + counts[1])

        with nc.Block() as block:
            @block.sync
            def _(sp):
                for dst, src in ((one_z, a["fft_one_z"]), (one_k, a["fft_one_k"]), (last, a["fft_last"]), (fwd, a["fft_fwd"]),
                                 (back, a["fft_back"]), (negt, a["hy_negt"])):
                    sp.dma_start(dst[:], src).then_inc(s_tab, 16)
                w = a["hy_w_in"][0].rearrange("(k p) (j c) -> p k j c", p=P, j=U_STEPS)
                lag = a["hy_filt_w_out"][0].rearrange("h (o d c) -> h o d c", o=ORDER, d=2)
                with sp.Fori(0, KT) as ct:
                    sp.wait_ge(s_up, 2 * U_STEPS * ct)
                    for j in range(U_STEPS):
                        sp.dma_start(w_in[:, :, j, :], w[:, :, j, bass.ds(ct * P, P)]).then_inc(s_w, 16)
                    for d in range(2):
                        sp.dma_start(w_lag[d * HID:(d + 1) * HID, :, :], lag[:, :, d, bass.ds(ct * P, P)]).then_inc(s_lagw, 16)
                    sp.wait_ge(s_exp_in, ct)
                    sp.dma_start(deltas[:, :], a["hy_deltas"][0, bass.ds(ct * P, P)].partition_broadcast(P)).then_inc(s_delta, 16)
                sp.wait_ge(s_up, 2 * U_STEPS * KT)
                sp.dma_start(m.aT[:, :, :], m.x_spill.rearrange("f p t -> p f t")).then_inc(s_back, 16)
                sp.wait_ge(s_back, 16)

            @block.gpsimd
            def _(pool):
                pool.wait_ge(s_tab, 16 * TABS)
                with pool.Fori(0, KT) as ct:
                    pool.wait_ge(s_delta, 16 * (ct + 1))
                    pool.wait_ge(s_dve, ct * sched.dve_turn)
                    pool.tensor_tensor(decay, negt[:, :].unsqueeze(2).to_broadcast([P, 16, P]),
                                       deltas[:, :].unsqueeze(1).to_broadcast([P, 16, P]), ALU.mult).then_inc(s_exp_in, 1)
                    pool.wait_ge(s_z, 2 * (ct + 1))
                    pool.dma_start(m.z_spill[bass.ds(ct, 1)].rearrange("o p t -> (o p) t"), zout[:, :]).then_inc(s_store, 16)
                pool.wait_ge(s_store, 16 * KT)

            def vector_at(which, col):
                return m.vec[which][:, bass.ds(col, 1)]

            def copy_out(name, k, ps):
                four = ps[:, :].rearrange("p (g c) -> p g c", g=4)
                if name == "S1f":
                    dst = eF.rearrange("p (s b g) -> p s b g", s=RA, g=16)[:, :, :, 4 * k:4 * k + 4]
                    return dst.rearrange("p s b g -> p (s b) g"), four.rearrange("p g c -> p c g")
                if name == "Tf":
                    return tF[:, 4 * k:4 * k + 4, :], four
                if name == "S2f":
                    n = 2 if k < 8 else 1
                    return (spec[:, 2 * k:2 * k + n, :, :].rearrange("p c i h -> p (c i h)"), ps[:, 0:n * 256])
                if name == "Tz":
                    return zt[:, 4 * k:4 * k + 4, :], four
                if name == "S1z":
                    dst = eZ.rearrange("p (s b g) -> p s b g", s=RA, g=8)[:, :, :, 2 * k:2 * k + 2]
                    return dst.rearrange("p s b g -> p (s b) g"), ps[:, :].rearrange("p (g c) -> p c g", g=2)
                if name in ("T2z", "Tv"):
                    return tZ[:, 4 * k:4 * k + 4, :], four
                assert name == "S3"
                return eZ[:, k * BANK:(k + 1) * BANK], ps[:, :]

            @block.scalar
            def _(act):
                with act.Fori(0, KT) as ct:
                    act.wait_ge(s_exp_in, ct + 1)
                    act.activation(decay, decay, ACT.Exp).then_inc(s_decay, 1)

                    def up_step(h):
                        j = h // 2
                        cols = slice((h % 2) * BANK, (h % 2 + 1) * BANK)
                        act.wait_ge(s_z, 2 * ct)
                        wait_apart(act, s_up, 2 * U_STEPS * ct + h + 1, s_apart)
                        if j == 3:
                            act.activation(gate[:, cols], up[j % 2][:, cols], ACT.Silu).then_inc(s_gate, 1)
                            return
                        act.activation(conv[:, j, cols], up[j % 2][:, cols], ACT.Identity,
                                       bias=vector_at(1, VEC_B["conv_b"] + j * KT + ct),
                                       scale=vector_at(1, VEC_B["conv_w"] + 24 + j * KT + ct)).then_inc(s_mid, 1)

                    for step in steps:
                        if step[0] == "U":
                            up_step(step[1])
                            continue
                        for k in range(sched.JOBS[step[0]]):
                            n = sched.first[step] + k
                            if sched.jobs[n][2]:
                                act.wait_ge(s_job, ct * NJ + n + 1)
                                dst, src = copy_out(step[0], k, bank[n % 4])
                                act.activation(dst, src, ACT.Copy).then_inc(s_act, 1)

            @block.vector
            def _(dve):
                with dve.Fori(0, KT) as ct:
                    def short(j):
                        dve.wait_ge(s_mid, 6 * ct + 2 * j + 2)
                        col = VEC_B["conv_w"] + j * KT + ct
                        dve.scalar_tensor_tensor(out=conv[:, j, 1:SEQ], in0=up[j % 2][:, 0:SEQ - 1], scalar=vector_at(1, col),
                                                 in1=conv[:, j, 1:SEQ], op0=ALU.mult, op1=ALU.add).then_inc(s_conv, 1)
                        dve.wait_ge(s_conv, 6 * ct + 2 * j + 1)
                        dve.scalar_tensor_tensor(out=conv[:, j, 0:SEQ - 1], in0=up[j % 2][:, 1:SEQ],
                                                 scalar=vector_at(1, col + 48), in1=conv[:, j, 0:SEQ - 1],
                                                 op0=ALU.mult, op1=ALU.add).then_inc(s_conv, 1)

                    def lags_out(k, ps):
                        if k == 0:
                            dve.wait_ge(s_decay, ct + 1)
                        return dve.tensor_tensor(kt[:, 4 * k:4 * k + 4, :], ps[:, :].rearrange("p (g c) -> p g c", g=4),
                                                 decay[:, 4 * k:4 * k + 4, :], ALU.mult)

                    def times_spectrum(k, ps):
                        c, n = 4 * k, min(4, 17 - 4 * k)
                        src = ps[:, 0:n * P].rearrange("p (c h) -> p c h", h=P)
                        dve.tensor_tensor(p1[:, c:c + n, :], src, spec[:, c:c + n, 0, :], ALU.mult)
                        return dve.tensor_tensor(p2[:, c:c + n, :], src, spec[:, c:c + n, 1, :], ALU.mult)

                    def finish(o, k, ps):
                        def half(t):
                            return t.rearrange("p (t g) -> p g t", g=16)[:, 8 * k:8 * k + 8, :]

                        src = ps[:, :].rearrange("p (g t) -> p g t", g=8)
                        dve.scalar_tensor_tensor(out=half(mix[:, :]), in0=half(conv[:, 0, :]),
                                                 scalar=vector_at(2, VEC_C["hy_bias"] + o * KT + ct), in1=src,
                                                 op0=ALU.mult, op1=ALU.add).then_inc(s_mix, 1)
                        if o == 1:
                            dve.wait_ge(s_mix, 6 * ct + 2 + 2 * k + 1)
                            dve.tensor_tensor(half(mix[:, :]), half(mix[:, :]), half(conv[:, 2, :]), ALU.mult).then_inc(s_mix, 1)
                            dve.wait_ge(s_mix, 6 * ct + 2 + 2 * k + 2)
                            dve.wait_ge(s_gate, 2 * (ct + 1))
                            dve.wait_ge(s_store, 16 * ct)
                            return dve.tensor_tensor(half(zout[:, :]), half(mix[:, :]), half(gate[:, :]), ALU.mult)
                        dve.wait_ge(s_mix, 6 * ct + k + 1)
                        return dve.tensor_tensor(half(conv[:, 0, :]), half(mix[:, :]), half(conv[:, 1, :]), ALU.mult)

                    for step in steps:
                        name, o = step
                        if name == "U":
                            if o in (1, 3, 5):
                                short(o // 2)
                            continue
                        if name == "S4":
                            dve.wait_ge(s_conv, 6 * ct + (4 if o == 0 else 6))
                        if name == "S2z":
                            wait_copied(dve, ct, (sched.after(("S2f", o))[0], 0))
                            dve.wait_ge(s_dve, ct * sched.dve_turn + sched.after(("S2f", o))[1])
                        for k in range(sched.JOBS[name]):
                            n = sched.first[step] + k
                            if sched.jobs[n][2]:
                                continue
                            ps = bank[n % 4]
                            dve.wait_ge(s_job, ct * NJ + n + 1)
                            if name == "K":
                                ins = lags_out(k, ps)
                            elif name == "S2z":
                                ins = times_spectrum(k, ps)
                            elif name == "S4":
                                ins = finish(o, k, ps)
                            else:
                                ins = dve.tensor_copy(*copy_out(name, k, ps))
                            ins.then_inc(s_dve, 1)
                            if name == "S4" and o == 1:
                                dve.wait_ge(s_dve, ct * sched.dve_turn + sched.copied(n + 1)[1])
                                dve.sem_inc(s_z, 1)

            @block.tensor
            def _(pe):
                pe.wait_ge(s_tab, 16 * TABS)
                with pe.Fori(0, KT) as ct:
                    def up_step(h):
                        j, cols = h // 2, slice((h % 2) * BANK, (h % 2 + 1) * BANK)
                        if h == 0:
                            pe.wait_ge(s_w, 16 * U_STEPS * (ct + 1))
                        if h % 2 == 0:
                            if j == 0:
                                pe.wait_ge(s_conv, 6 * ct)
                            elif j == 1:
                                pe.wait_ge(s_gate, 2 * ct)
                            else:
                                pe.wait_ge(s_conv, 6 * ct + 2 * (j - 1))
                        for k in range(KT):
                            mm = pe.matmul(up[j % 2][:, cols], w_in[:, k, j, :], m.aT[:, k, cols],
                                           start=(k == 0), stop=(k == KT - 1))
                        mm.then_inc(s_up, 1)

                    def products(name, o, k, ps):
                        if name == "K":
                            for i in range(4):
                                mm = pe.matmul(ps[:, i * P:(i + 1) * P], m.lags[:, 4 * k + i:NFFT:16], w_lag[:, o, :],
                                               start=True, stop=True)
                        elif name == "S1f":
                            for i in range(4):
                                mm = pe.matmul(ps[:, i * P:(i + 1) * P], kt[:, 4 * k + i, :], one_k[:, :], start=True, stop=True)
                        elif name in ("Tf", "T2z"):
                            src = eF if name == "Tf" else eZ
                            for i in range(4):
                                mm = pe.transpose(ps[:, i * P:(i + 1) * P], src[:, (4 * k + i) * P:(4 * k + i + 1) * P],
                                                  m.ident[:, :])
                        elif name == "S2f":
                            for i in range(4 if k < 8 else 2):
                                c = 2 * k + i // 2
                                mm = pe.matmul(ps[:, i * P:(i + 1) * P], fwd[:, c, (i % 2) * P:(i % 2 + 1) * P],
                                               tF[:, c % 16, :], start=True, stop=True)
                        elif name == "Tz":
                            for i in range(4):
                                mm = pe.transpose(ps[:, i * P:(i + 1) * P], conv[:, 0, 4 * k + i:SEQ:8], m.ident[:, :])
                        elif name == "S1z":
                            for i in range(2):
                                mm = pe.matmul(ps[:, i * 256:(i + 1) * 256], zt[:, 2 * k + i, :], one_z[:, :],
                                               start=True, stop=True)
                        elif name == "S2z":
                            for i in range(min(4, 17 - 4 * k)):
                                c = 4 * k + i
                                mm = pe.matmul(ps[:, i * P:(i + 1) * P], fwd[:, c, 64:192], tZ[:, c % 16, :],
                                               start=True, stop=True)
                        elif name == "S3":
                            for i in range(4):
                                c = 4 * k + i
                                for s, col, n in ((0, 0, 64), (16, 64, 64)) if c == 0 else ((c, 0, P),):
                                    o_ = ps[:, i * P + col:i * P + col + n]
                                    pe.matmul(o_, p1[:, s, :], back[:, s, 64:64 + n], start=True, stop=False)
                                    mm = pe.matmul(o_, p2[:, s, :], back[:, s, 0:n], start=False, stop=True)
                        elif name == "Tv":
                            for i in range(4):
                                mm = pe.transpose(ps[:, i * P:(i + 1) * P], eZ[:, 4 * k + i:2048:16], m.ident[:, :])
                        else:
                            assert name == "S4"
                            for i in range(8):
                                mm = pe.matmul(ps[:, i * 64:(i + 1) * 64], tZ[:, 8 * k + i, :], last[:, :], start=True, stop=True)
                        return mm

                    source = dict(S1f="K", Tf="S1f", S2f="Tf", S1z="Tz", T2z="S1z", S2z="T2z", S3="S2z", Tv="S3", S4="Tv")
                    for step in steps:
                        name, o = step
                        if name == "U":
                            up_step(o)
                            continue
                        if name == "K" and o == 0:
                            pe.wait_ge(s_lagw, 32 * (ct + 1))
                        if name == "Tz" and o == 0:
                            pe.wait_ge(s_conv, 6 * ct + 2)
                        if name == "Tz" and o == 1:
                            wait_copied(pe, ct, (0, sched.after(("S4", 0))[1]))
                        if name in source:
                            wait_copied(pe, ct, sched.after((source[name], o)))
                        for k in range(sched.JOBS[name]):
                            n = sched.first[step] + k
                            if n >= 4:
                                by_act = sched.jobs[n - 4][2]
                                wait_copied(pe, ct, tuple(x if by_act == (i == 0) else 0
                                                          for i, x in enumerate(sched.copied(n - 3))))
                            else:
                                pe.wait_ge(s_act, ct * sched.act_turn)
                                pe.wait_ge(s_dve, ct * sched.dve_turn)
                            products(name, o, k, bank[n % 4]).then_inc(s_job, 1)


def hyena_layer(nc, m, a, ctx, out):
    m.x_spill = nc.dram_tensor("x_spill", (KT, P, SEQ), F32, kind="Internal").ap()
    m.z_spill = nc.dram_tensor("z_spill", (KT, P, SEQ), F32, kind="Internal").ap()
    m.aT = ctx.enter_context(nc.sbuf_tensor("aT", [P, KT, SEQ], F32))
    with ExitStack() as c:
        m.lags = c.enter_context(nc.sbuf_tensor("lags", [P, NFFT], F32))
        hyena_prepare(nc, m, a)
        hyena_convolve(nc, m, a)
    m.xT, m.aT = m.aT, m.xT
    chunks = [m.ring.plan((slot_cols(512), weight_cols(a["hy_w_out"][0], 512 * j, 512 * j + 512))) for j in range(2)]
    m.prefetch = lambda sp: m.ring.send(sp, chunks[-1])
    add_product(nc, m, chunks, m.aT, "hy_out", lambda f: m.ada[:, 1, 16 + f, 0:1], m.z_spill)


def second_norms(nc, m, a, ctx, out):
    m.lb = ctx.enter_context(nc.sbuf_tensor("lb", [P, 2, HG_HEADS], F32))
    with Stage(nc, "b2_in") as st:
        norm = RmsNorm(st, m, SEQ)
        n_final, n_first = norm.plan(KT, SEQ, D), norm.plan(KT, SEQ, D)
        top, ex, tot = st.sb("top", [P, HG_HEADS]), st.sb("ex", [P, 2, HG_HEADS]), st.sb("tot", [P, 2, HG_HEADS])
        s_x, s_a, s_lb, s_exp = st.sem("x"), st.sem("a"), st.sem("lower"), st.sem("exp")
        with nc.Block() as block:
            @block.scalar
            def _(act):
                act.wait_ge(s_lb, 3)
                act.activation(ex[:, :, :], ex[:, :, :], ACT.Exp).then_inc(s_exp, 1)
                norm.square(act, n_final, lambda f: m.xT[:, f, :])
                norm.root(act, n_final)
                act.wait_ge(s_x, KT)
                norm.square(act, n_first, lambda f: m.xT[:, f, :])
                norm.root(act, n_first)

            @block.tensor
            def _(pe):
                norm.total(pe, n_final)
                norm.spread(pe, n_final)
                norm.total(pe, n_first)
                pe.wait_ge(s_x, KT)
                norm.spread(pe, n_first)

            @block.vector
            def _(dve):
                rows = [m.vec[2][:, VEC_C["hgrn_lb"] + r * HG_HEADS:][:, 0:HG_HEADS] for r in range(2)]
                dve.tensor_tensor(top[:, :], rows[0], rows[1], ALU.max).then_inc(s_lb, 1)
                dve.wait_ge(s_lb, 1)
                for r in range(2):
                    dve.tensor_tensor(ex[:, r, :], rows[r], top[:, :], ALU.subtract).then_inc(s_lb, 1)
                dve.wait_ge(s_exp, 1)
                dve.tensor_tensor(tot[:, 0, :], ex[:, 0, :], ex[:, 1, :], ALU.add).then_inc(s_lb, 1)
                dve.wait_ge(s_lb, 4)
                dve.reciprocal(tot[:, 1, :], tot[:, 0, :]).then_inc(s_lb, 1)
                dve.wait_ge(s_lb, 5)
                dve.tensor_tensor(m.lb[:, 0, :], ex[:, 0, :], tot[:, 1, :], ALU.mult).then_inc(s_lb, 1)
                dve.wait_ge(s_lb, 6)
                dve.tensor_scalar(m.lb[:, 1, :], m.lb[:, 0, :], -1.0, 1.0, ALU.mult, ALU.add).then_inc(s_lb, 1)
                for k, g, dst, sem in ((n_final, m.vec[0][:, VEC_A["final_g"]:], m.xT, s_x),
                                       (n_first, m.vec[2][:, VEC_C["norm1_w"]:], m.aT, s_a)):
                    norm.invert(dve, k)
                    norm.wait_spread(dve, k)
                    for f in range(KT):
                        dve.scalar_tensor_tensor(out=dst[:, f, :], in0=m.xT[:, f, :], scalar=g[:, f:f + 1],
                                                 in1=norm.rb[:, 0:SEQ], op0=ALU.mult, op1=ALU.mult).then_inc(sem, 1)
                dve.wait_ge(s_a, KT)


def window_attention(nc, m, a):
    QW, HEADS, HALF = QH * HD, QH + KVH, ROT // 2
    ring = m.ring
    w_q = ring.plan((slot_cols(512), weight_cols(a["w_in_2"][0], 0, QW)))
    w_kv = ring.plan((slot_cols(256), weight_cols(a["w_in_2"][0], QW, QW + 2 * KVH * HD)))
    TWO_PI = (6.28125, 0.0019350051879882812, 3.019915981956753e-07)
    MAGIC, PI_DOWN = 1.5 * 2.0 ** 23, 3.1415925
    MASKED = -1e30
    with Stage(nc, "swa") as st:
        pos_i, pos_f = st.sb("pos_i", [TT, P], I32), st.sb("pos_f", [TT, P])
        pos, ang = st.sb("pos", [P, TT]), st.sb("ang", [P, 2, TT, HALF])
        inv_freq, turns = st.sb("inv_freq", [P, HALF]), st.sb("turns", [P, 2, TT, HALF])
        trig = st.sb("trig", [P, 2, TT, HALF])
        norm_w, sink = st.sb("norm_w", [P, 2, HD]), st.sb("sink", [P, QH])
        mask = st.sb("mask", [P, 2, P])
        first = st.sb("first", [P, 2, P])
        x_blk = st.sb("x_blk", [P, 2, KT, P])
        qk, sq = st.sb("qk", [P, 2, HEADS, HD]), st.sb("sq", [P, HEADS, HD])
        var, inv = st.sb("var", [P, 2, HEADS]), st.sb("inv", [P, 2, HEADS])
        rope = st.sb("rope", [P, 4, HEADS, HALF])
        qT, kT, v = st.sb("qT", [P, 4, P]), st.sb("kT", [P, 3, P]), st.sb("v", [P, 3, P])
        s_sb, pT = st.sb("s", [P, QH, 2, P]), st.sb("pT", [P, QH, 2, P])
        top, neg, den, ext, nsink = (st.sb(n, [P, QH]) for n in ("top", "neg", "den", "ext", "nsink"))
        v_new = st.sb("v_new", [P, 2, P])
        proj, feat = st.ps("proj", 2 * BANK), st.ps("feat", 2 * BANK)
        work = [st.ps(f"work{i}", 2 * BANK) for i in range(2)]
        s_in, s_pos, s_tab, s_sin = st.sem("in"), st.sem("pos"), st.sem("table"), st.sem("sine")
        s_blk, s_proj, s_copy, s_norm, s_root = (st.sem(n) for n in ("block", "projected", "copied", "normed", "root"))
        s_turn, s_feat, s_score, s_soft, s_exp = (st.sem(n) for n in ("turned", "features", "scores", "softmax", "exp"))
        s_pturn, s_pcopy, s_out, s_done, s_first, s_k, s_v, s_apart = (st.sem(n) for n in ("p_turned", "p_copied", "out", "done", "first", "k_moved", "v_moved", "apart"))
        NORM, SOFT, EXP, TURNS = 13, 8, QH + 1, TT // 2
        s_none = st.sem("none")

        with nc.Block() as block:
            @block.sync
            def _(sp):
                ring.send(sp, w_kv)
                sp.dma_start(pos_i[:, :], a["positions_2"][0].rearrange("(t p) -> t p", p=P)).then_inc(s_in, 16)
                sp.dma_start(inv_freq[:, :], a["swa_inv_freq"][0].partition_broadcast(P)).then_inc(s_in, 16)
                sp.dma_start(norm_w[:, 0, :], a["q_norm_w_2"][0].partition_broadcast(P)).then_inc(s_in, 16)
                sp.dma_start(norm_w[:, 1, :], a["k_norm_w_2"][0].partition_broadcast(P)).then_inc(s_in, 16)
                sp.dma_start(sink[:, :], a["attn_sinks_2"][0].partition_broadcast(P)).then_inc(s_in, 16)
                sp.dma_start(mask[:, :, :], a["swa_mask"]).then_inc(s_in, 16)

            @block.gpsimd
            def _(pool):
                pool.wait_ge(s_in, 16 * 6)
                pool.tensor_copy(first[:, 1, :], mask[:, 1, :]).then_inc(s_first, 1)
                pool.memset(first[:, 0, :], MASKED).then_inc(s_first, 1)
                pool.memset(kT[:, 2, :], 0.0).then_inc(s_none, 1)
                pool.memset(v[:, 2, :], 0.0).then_inc(s_none, 1)
                pool.wait_ge(s_none, 2)

                def turn(pair):
                    wait_apart(pool, s_score, 2 * pair, s_apart)
                    pool.tensor_copy(kT[:, 0, :], kT[:, 2, :]).then_inc(s_k, 1)
                    wait_apart(pool, s_out, 2 * pair, s_apart)
                    pool.tensor_copy(v[:, 0, :], v[:, 2, :]).then_inc(s_v, 1)
                    wait_apart(pool, s_copy, 6 * pair + 6, s_apart)
                    wait_apart(pool, s_v, 3 * pair + 1, s_apart)
                    for b in range(2):
                        pool.tensor_copy(v[:, b + 1, :], v_new[:, b, :]).then_inc(s_v, 1)
                    wait_apart(pool, s_soft, 2 * SOFT * pair + 1, s_apart)
                    pool.tensor_copy(first[:, 0, :], mask[:, 0, :]).then_inc(s_first, 1)

                with pool.Fori(0, TURNS) as pair:
                    turn(pair)

            @block.scalar
            def _(act):
                act.wait_ge(s_tab, 12)
                act.activation(trig[:, :, :, :], ang[:, :, :, :], ACT.Sin).then_inc(s_sin, 1)

                def take(pair):
                    for b in range(2):
                        act.activation(x_blk[:, b, :, :], m.aT[:, :, bass.ds(pair * (2 * P) + b * P, P)], ACT.Copy).then_inc(s_blk, 1)

                def project(n, b):
                    act.wait_ge(s_proj, n + 1)
                    act.activation(qk[:, b, 0:QH, :].rearrange("p (j g) d -> p j g d", g=2),
                                   proj[:, 0:QW].rearrange("p (g j d) -> p j g d", g=2, d=HD), ACT.Copy).then_inc(s_copy, 1)
                    act.activation(qk[:, b, QH:HEADS, :].rearrange("p g d -> p (g d)"),
                                   proj[:, QW:QW + P], ACT.Copy).then_inc(s_copy, 1)
                    act.activation(v_new[:, b, :], proj[:, QW + P:QW + 2 * P], ACT.Copy).then_inc(s_copy, 1)

                def root(n, b):
                    act.wait_ge(s_norm, NORM * n + 3)
                    act.activation(inv[:, b, :], var[:, b, :], ACT.Sqrt).then_inc(s_root, 1)

                take(0)
                for b in range(2):
                    project(b, b)
                    root(b, b)

                def turn(pair, more):
                    if more:
                        wait_apart(act, s_proj, 2 * pair + 2, s_apart)
                        take(pair + 1)
                    for b in range(2):
                        n = 2 * pair + b
                        act.wait_ge(s_turn, n + 1)
                        act.wait_ge(s_score, n)
                        act.wait_ge(s_k, pair + 1)
                        act.activation(qT[:, :, :], feat[:, 0:QW].rearrange("p (j q) -> p j q", q=P), ACT.Copy).then_inc(s_feat, 1)
                        act.activation(kT[:, b + 1, :], feat[:, QW:QW + P], ACT.Copy).then_inc(s_feat, 1)
                        act.wait_ge(s_soft, SOFT * n + 4)
                        for h in range(QH):
                            act.activation(s_sb[:, h, :, :], s_sb[:, h, :, :], ACT.Exp, bias=neg[:, h:h + 1],
                                           accum_out=den[:, h:h + 1]).then_inc(s_exp, 1)
                        act.activation(ext[:, :], ext[:, :], ACT.Exp).then_inc(s_exp, 1)
                        if more:
                            act.wait_ge(s_v, 3 * pair + 3)
                            project(n + 2, b)
                        for i in range(2):
                            act.wait_ge(s_out, n)
                            act.wait_ge(s_pturn, 2 * n + i + 1)
                            act.activation(pT[:, 4 * i:4 * i + 4, :, :].rearrange("p h k q -> p (h k q)"),
                                           work[i][:, :], ACT.Copy).then_inc(s_pcopy, 1)
                        if more:
                            root(n + 2, b)
                        wait_apart(act, s_out, n + 1, s_apart)
                        for g in range(2):
                            rows = slice(HD * g, HD * g + HD)
                            act.activation(m.attnT[rows, :, bass.ds(n * P, P)],
                                           feat[rows, g * BANK:(g + 1) * BANK].rearrange("p (j q) -> p j q", q=P),
                                           ACT.Copy).then_inc(s_done, 1)

                with act.Fori(0, TURNS - 1) as pair:
                    turn(pair, True)
                turn(TURNS - 1, False)

            @block.vector
            def _(dve):
                dve.wait_ge(s_in, 16 * 6)
                dve.tensor_copy(pos_f[:, :], pos_i[:, :]).then_inc(s_pos, 1)
                dve.wait_ge(s_pos, 2)
                dve.tensor_copy(pos[:, :], proj[:, 0:TT]).then_inc(s_tab, 1)
                dve.wait_ge(s_tab, 1)
                for i in range(2):
                    dve.tensor_tensor(ang[:, i, :, :], pos[:, :].unsqueeze(2).to_broadcast([P, TT, HALF]),
                                      inv_freq[:, :].unsqueeze(1).to_broadcast([P, TT, HALF]), ALU.mult).then_inc(s_tab, 1)
                dve.wait_ge(s_tab, 3)
                for i in range(2):
                    dve.tensor_scalar(turns[:, i, :, :], ang[:, i, :, :], 1.0 / (2.0 * np.pi), 0.25 * (1 - i), ALU.mult, ALU.add)\
                       .then_inc(s_tab, 1)
                for i, op in enumerate((ALU.add, ALU.subtract)):
                    dve.wait_ge(s_tab, 5 + i)
                    dve.tensor_scalar(turns[:, :, :, :], turns[:, :, :, :], MAGIC, None, op).then_inc(s_tab, 1)
                for i, part in enumerate(TWO_PI):
                    dve.wait_ge(s_tab, 7 + i)
                    dve.scalar_tensor_tensor(out=ang[:, :, :, :], in0=turns[:, :, :, :], scalar=-part, in1=ang[:, :, :, :],
                                             op0=ALU.mult, op1=ALU.add).then_inc(s_tab, 1)
                dve.wait_ge(s_tab, 10)
                dve.tensor_scalar(ang[:, 0, :, :], ang[:, 0, :, :], np.pi / 2, None, ALU.add).then_inc(s_tab, 1)
                dve.wait_ge(s_tab, 11)
                dve.tensor_scalar(ang[:, :, :, :], ang[:, :, :, :], PI_DOWN, -PI_DOWN, ALU.min, ALU.max).then_inc(s_tab, 1)
                dve.tensor_scalar(nsink[:, :], sink[:, :], -1.0, None, ALU.mult).then_inc(s_pos, 1)
                dve.wait_ge(s_pos, 3)
                dve.wait_ge(s_sin, 1)

                def normed(n, b):
                    at = NORM * n
                    x = qk[:, b, :, :]
                    dve.wait_ge(s_copy, 3 * n + 2)
                    dve.tensor_tensor(sq[:, :, :], x, x, ALU.mult).then_inc(s_norm, 1)
                    dve.wait_ge(s_norm, at + 1)
                    dve.tensor_reduce(var[:, b, :], sq[:, :, :], AX.X, ALU.add).then_inc(s_norm, 1)
                    dve.wait_ge(s_norm, at + 2)
                    dve.tensor_scalar(var[:, b, :], var[:, b, :], 1.0 / HD, EPS, ALU.mult, ALU.add).then_inc(s_norm, 1)
                    dve.wait_ge(s_root, n + 1)
                    dve.reciprocal(inv[:, b, :], inv[:, b, :]).then_inc(s_norm, 1)
                    dve.wait_ge(s_norm, at + 4)
                    dve.tensor_tensor(x, x, inv[:, b, :].unsqueeze(2).to_broadcast([P, HEADS, HD]), ALU.mult).then_inc(s_norm, 1)
                    dve.wait_ge(s_norm, at + 5)
                    for i, (lo, hi) in enumerate(((0, QH), (QH, HEADS))):
                        dve.tensor_tensor(x[:, lo:hi, :], x[:, lo:hi, :],
                                          norm_w[:, i, :].unsqueeze(1).to_broadcast([P, hi - lo, HD]), ALU.mult).then_inc(s_norm, 1)
                    dve.wait_ge(s_norm, at + 7)
                    cos, sin = (trig[:, i, bass.ds(n, 1), :].to_broadcast([P, HEADS, HALF]) for i in range(2))
                    x1, x2 = x[:, :, 0:HALF], x[:, :, HALF:ROT]
                    for i, (u, w) in enumerate(((x1, cos), (x2, sin), (x2, cos), (x1, sin))):
                        dve.tensor_tensor(rope[:, i, :, :], u, w, ALU.mult).then_inc(s_norm, 1)
                    dve.wait_ge(s_norm, at + 11)
                    dve.tensor_tensor(x1, rope[:, 0, :, :], rope[:, 1, :, :], ALU.subtract).then_inc(s_norm, 1)
                    dve.tensor_tensor(x2, rope[:, 2, :, :], rope[:, 3, :, :], ALU.add).then_inc(s_norm, 1)
                    dve.wait_ge(s_norm, at + 13)

                for b in range(2):
                    normed(b, b)

                def turn(pair, more):
                    for b in range(2):
                        n = 2 * pair + b
                        at = SOFT * n
                        flat = s_sb[:, :, :, :].rearrange("p h k q -> p h (k q)")
                        mask_b = (mask if b else first)[:, :, :].rearrange("p k q -> p (k q)").unsqueeze(1).to_broadcast([P, 4, 2 * P])
                        if b == 0:
                            dve.wait_ge(s_first, 2 + pair)
                        dve.wait_ge(s_pturn, 2 * n)
                        for i in range(2):
                            dve.wait_ge(s_score, n + 1)
                            ins = dve.scalar_tensor_tensor(out=flat[:, 4 * i:4 * i + 4, :], in0=work[i][:, :].rearrange("p (h k) -> p h k", h=4),
                                                           scalar=HD ** -0.5, in1=mask_b, op0=ALU.mult, op1=ALU.add)
                        ins.then_inc(s_soft, 1)
                        dve.wait_ge(s_soft, at + 1)
                        dve.tensor_reduce(top[:, :], flat, AX.X, ALU.max).then_inc(s_soft, 1)
                        dve.wait_ge(s_soft, at + 2)
                        dve.scalar_tensor_tensor(out=neg[:, :], in0=top[:, :], scalar=-1.0, in1=nsink[:, :], op0=ALU.mult, op1=ALU.min)\
                           .then_inc(s_soft, 1)
                        dve.wait_ge(s_soft, at + 3)
                        dve.tensor_tensor(ext[:, :], sink[:, :], neg[:, :], ALU.add).then_inc(s_soft, 1)
                        dve.wait_ge(s_exp, EXP * (n + 1))
                        dve.tensor_tensor(den[:, :], den[:, :], ext[:, :], ALU.add).then_inc(s_soft, 1)
                        dve.wait_ge(s_soft, at + 5)
                        dve.reciprocal(top[:, :], den[:, :]).then_inc(s_soft, 1)
                        dve.wait_ge(s_soft, at + 6)
                        for i in range(2):
                            dve.tensor_tensor(flat[:, 4 * i:4 * i + 4, :], flat[:, 4 * i:4 * i + 4, :],
                                              top[:, 4 * i:4 * i + 4].unsqueeze(2).to_broadcast([P, 4, 2 * P]), ALU.mult).then_inc(s_soft, 1)
                        if more:
                            normed(n + 2, b)

                with dve.Fori(0, TURNS - 1) as pair:
                    turn(pair, True)
                turn(TURNS - 1, False)

            @block.tensor
            def _(pe):
                pe.wait_ge(s_pos, 1)
                pe.transpose(proj[:, 0:TT], pos_f[:, :], m.ident[0:TT, 0:TT]).then_inc(s_pos, 1)
                pe.wait_ge(*ring.landed_at(w_q))
                pe.wait_ge(*ring.landed_at(w_kv))
                wq = ring.slot(w_q)[:, :].rearrange("p (k c) -> p k c", k=KT)
                wkv = ring.slot(w_kv)[:, 0:KT * 256].rearrange("p (k c) -> p k c", k=KT)
                pe.wait_ge(s_tab, 1)

                def project(n, b):
                    pe.wait_ge(s_blk, n + 1)
                    pe.wait_ge(s_copy, 3 * n)
                    for k in range(KT):
                        pe.matmul(proj[:, 0:QW], x_blk[:, b, k, :], wq[:, k, :], start=(k == 0), stop=(k == KT - 1))
                    for k in range(KT):
                        mm = pe.matmul(proj[:, QW:QW + 256], x_blk[:, b, k, :], wkv[:, k, :], start=(k == 0), stop=(k == KT - 1))
                    mm.then_inc(s_proj, 1)

                for b in range(2):
                    project(b, b)

                def turn(pair, more):
                    for b in range(2):
                        n = 2 * pair + b
                        pe.wait_ge(s_norm, NORM * (n + 1))
                        pe.wait_ge(s_done, 2 * n)
                        for j in range(5):
                            mm = pe.transpose(feat[:, j * P:(j + 1) * P],
                                              qk[:, b, 2 * j:2 * j + 2, :].rearrange("p g d -> p (g d)"), m.ident[:, :])
                        mm.then_inc(s_turn, 1)
                        pe.wait_ge(s_feat, 2 * (n + 1))
                        pe.wait_ge(s_pcopy, 2 * n)
                        for h in range(QH):
                            g, j = h // 4, h % 4
                            mm = pe.matmul(work[g][:, j * 256:(j + 1) * 256], qT[HD * g:HD * g + HD, j, :],
                                           kT[HD * g:HD * g + HD, b:b + 2, :].rearrange("p k q -> p (k q)"), start=True, stop=True)
                        mm.then_inc(s_score, 1)
                        if more:
                            project(n + 2, b)
                        for i in range(2):
                            pe.wait_ge(s_soft, SOFT * n + 7 + i)
                            for j in range(8):
                                mm = pe.transpose(work[i][:, j * P:(j + 1) * P], s_sb[:, 4 * i + j // 2, j % 2, :], m.ident[:, :])
                            mm.then_inc(s_pturn, 1)
                        pe.wait_ge(s_pcopy, 2 * n + 2)
                        pe.wait_ge(s_v, 3 * pair + 3)
                        for h in range(QH):
                            for k in range(2):
                                mm = pe.matmul(feat[:, h * P:(h + 1) * P], v[:, b + k, :], pT[:, h, k, :],
                                               start=(k == 0), stop=(k == 1))
                        mm.then_inc(s_out, 1)

                with pe.Fori(0, TURNS - 1) as pair:
                    turn(pair, True)
                turn(TURNS - 1, False)
                pe.wait_ge(s_proj, TT)
                pe.sem_inc(ring.used, 2)


def gated_recurrence(nc, m, a):
    LEVELS = 7
    KINDS = ("f", "q", "g", "v")
    COLUMN = dict(q=768, f=1280, v=1792, g=2304)
    HALVES = SEQ // BANK
    with Stage(nc, "hgrn") as st:
        w = m.ring.slots[0][:, :].rearrange("p (j k c) -> p j k c", j=4, k=KT)
        v, kRt, AT, S = (m.ring.slots[2][:, i * SEQ:(i + 1) * SEQ].rearrange("p (c t) -> p c t", c=TT) for i in range(4))
        F, R, k, q = (st.sb(n, [P, SEQ]) for n in ("F", "R", "k", "q"))
        K, Q = st.sb("K", [P, 2, SEQ]), st.sb("Q", [P, 2, SEQ])
        mask = st.sb("mask", [P, LEVELS + 1, P], I32)
        proj = [st.ps(f"proj{i}") for i in range(4)]
        work = [st.ps(f"work{i}") for i in range(4)]
        s_w = {n: st.sem(f"w_{n}") for n in KINDS}
        s_mask, s_zero, s_proj, s_sig, s_q = (st.sem(n) for n in ("mask", "zero", "projected", "sigmoid", "q"))
        s_g, s_v, s_gate, s_decay, s_kq = (st.sem(n) for n in ("g", "v", "gate", "decay", "kq"))
        s_a, s_sel, s_turn, s_krt, s_kv = (st.sem(n) for n in ("a", "selected", "turned", "krt", "kv"))
        s_state, s_o, s_out, s_apart = st.sem("state"), st.sem("o"), st.sem("out"), st.sem("apart")
        PROJ, DECAY, KQ, A, STATE = 8, 1 + 2 * LEVELS, 1 + 2 * (LEVELS - 1) + 2, 2 * (LEVELS + 1), TT - 1

        def blocks(t, level):
            return t.rearrange("p (b two m) -> p b two m", two=2, m=1 << (level - 1))

        def kq_at(level):
            return 1 + 2 * (level - 1)

        with nc.Block() as block:
            @block.sync
            def _(sp):
                sp.dma_start(mask[:, :, :], a["hg_mask"]).then_inc(s_mask, 16)
                with sp.Fori(0, HG_HEADS) as h:
                    for j, n in enumerate(KINDS):
                        sp.wait_ge(s_proj, PROJ * h)
                        src = a["w_in_2"][0].rearrange("(k p) c -> p k c", p=P)
                        sp.dma_start(w[:, j, :, :], src[:, :, bass.ds(COLUMN[n] + h * P, P)]).then_inc(s_w[n], 16)

            @block.tensor
            def _(pe):
                pe.wait_ge(s_zero, 5)
                with pe.Fori(0, HG_HEADS) as h:
                    def feature_major(n, half):
                        bank = proj[2 * (n == "q") + half]
                        for kt in range(KT):
                            mm = pe.matmul(bank[:, :], w[:, KINDS.index(n), kt, :], m.aT[:, kt, half * BANK:(half + 1) * BANK],
                                           start=(kt == 0), stop=(kt == KT - 1))
                        mm.then_inc(s_proj, 1)

                    def values(t):
                        for kt in range(KT):
                            mm = pe.matmul(proj[2 + t // 4][:, (t % 4) * P:(t % 4 + 1) * P], m.aT[:, kt, t * P:(t + 1) * P],
                                           w[:, 3, kt, :], start=(kt == 0), stop=(kt == KT - 1))
                        if t % 4 == 3:
                            mm.then_inc(s_proj, 1)

                    pe.wait_ge(s_w["f"], 16 * h + 16)
                    pe.wait_ge(s_krt, 2 * h)
                    for half in range(2):
                        feature_major("f", half)
                    pe.wait_ge(s_w["q"], 16 * h + 16)
                    pe.wait_ge(s_state, STATE * h)
                    for half in range(2):
                        feature_major("q", half)
                    pe.wait_ge(s_q, 2 * h + 2)
                    pe.wait_ge(s_gate, 2 * h + 2)
                    for level in range(LEVELS + 1):
                        if level:
                            pe.wait_ge(s_kq, KQ * h + kq_at(level))
                        for half in range(2):
                            i = 2 * level + half
                            if i < 2:
                                pe.wait_ge(s_out, 2 * h)
                            pe.wait_ge(s_sel, A * h + max(i - 3, 0))
                            for c in range(4):
                                cols = slice(half * BANK + c * P, half * BANK + (c + 1) * P)
                                left = k[:, cols] if level < 2 else K[:, level % 2, cols]
                                right = q[:, cols] if level == 0 else Q[:, level % 2, cols]
                                mm = pe.matmul(work[i % 4][:, c * P:(c + 1) * P], left, right, start=True, stop=True)
                            mm.then_inc(s_a, 1)
                        if level < 2:
                            if level == 0:
                                pe.wait_ge(s_w["g"], 16 * h + 16)
                                pe.wait_ge(s_sig, 2 * h + 2)
                            feature_major("g", level)
                        else:
                            if level == 2:
                                pe.wait_ge(s_w["v"], 16 * h + 16)
                            for t in range((level - 2) * TT // 6, (level - 1) * TT // 6):
                                values(t)
                    pe.wait_ge(s_kq, KQ * (h + 1))
                    pe.wait_ge(s_g, 2 * h + 2)
                    for half in range(2):
                        for c in range(4):
                            at = half * BANK + c * P
                            mm = pe.transpose(proj[half][:, c * P:(c + 1) * P], K[:, 0, at:at + P], m.ident[:, :])
                        mm.then_inc(s_turn, 1)
                    pe.wait_ge(s_krt, 2 * h + 2)
                    pe.wait_ge(s_v, 2 * h + 2)
                    for c in range(TT - 1):
                        mm = pe.matmul(proj[2 + c // 4][:, (c % 4) * P:(c % 4 + 1) * P], kRt[:, c, :], v[:, c, :], start=True, stop=True)
                    mm.then_inc(s_kv, 1)
                    pe.wait_ge(s_sel, A * (h + 1))
                    pe.wait_ge(s_state, STATE * (h + 1))
                    for c in range(TT):
                        o = work[c // 4][:, (c % 4) * P:(c % 4 + 1) * P]
                        mm = pe.matmul(o, v[:, c, :], AT[:, c, :], start=True, stop=(c == 0))
                        if c:
                            mm = pe.matmul(o, S[:, c, :], Q[:, 0, c * P:(c + 1) * P], start=False, stop=True)
                        if c % 4 == 3:
                            mm.then_inc(s_o, 1)

            @block.scalar
            def _(act):
                with act.Fori(0, HG_HEADS) as h:
                    act.wait_ge(s_state, STATE * h)
                    act.wait_ge(s_kq, KQ * h)
                    act.wait_ge(s_decay, DECAY * h)
                    act.wait_ge(s_a, A * h)
                    for half in range(2):
                        act.wait_ge(s_proj, PROJ * h + half + 1)
                        act.activation(F[:, half * BANK:(half + 1) * BANK], proj[half][:, :], ACT.Sigmoid).then_inc(s_sig, 1)
                    for half in range(2):
                        act.wait_ge(s_proj, PROJ * h + half + 3)
                        act.activation(q[:, half * BANK:(half + 1) * BANK], proj[2 + half][:, :], ACT.Silu).then_inc(s_q, 1)
                    for half in range(2):
                        act.wait_ge(s_proj, PROJ * h + half + 5)
                        act.activation(m.silu_g[:, bass.ds(h, 1), half * BANK:(half + 1) * BANK].rearrange("p o t -> p (o t)"),
                                       proj[half][:, :], ACT.Silu).then_inc(s_g, 1)
                    act.wait_ge(s_o, 2 * h)
                    for half in range(2):
                        act.wait_ge(s_proj, PROJ * h + half + 7)
                        act.activation(v[:, 4 * half:4 * half + 4, :].rearrange("p c t -> p (c t)"), proj[2 + half][:, :], ACT.Copy)\
                           .then_inc(s_v, 1)
                    for half in range(2):
                        act.wait_ge(s_turn, 2 * h + half + 1)
                        act.activation(kRt[:, 4 * half:4 * half + 4, :].rearrange("p c t -> p (c t)"), proj[half][:, :], ACT.Copy)\
                           .then_inc(s_krt, 1)
                    for half in range(2):
                        act.wait_ge(s_o, 2 * h + half + 1)
                        act.activation(m.hgrnT[:, bass.ds(h, 1), half * BANK:(half + 1) * BANK].rearrange("p o t -> p (o t)"),
                                       work[half][:, :], ACT.Copy).then_inc(s_out, 1)

            @block.gpsimd
            def _(pool):
                pool.memset(AT[:, :, :], 0.0).then_inc(s_zero, 1)
                for i in range(2):
                    pool.memset(K[:, i, :], 0.0).then_inc(s_zero, 1)
                    pool.memset(Q[:, i, :], 0.0).then_inc(s_zero, 1)
                with pool.Fori(0, HG_HEADS) as h:
                    wait_apart(pool, s_kq, KQ * h, s_apart)
                    pool.memset(R[:, :], 1.0).then_inc(s_decay, 1)
                    pool.wait_ge(s_gate, 2 * h + 2)
                    for level in range(1, LEVELS + 1):
                        Fb, Rb = blocks(F[:, :], level), blocks(R[:, :], level)
                        mm = 1 << (level - 1)
                        shape = [P, SEQ // (2 * mm), mm]
                        pool.wait_ge(s_kq, KQ * h + kq_at(level))
                        pool.wait_ge(s_decay, DECAY * h + 1 + 2 * (level - 1))
                        pool.tensor_tensor(Rb[:, :, 0, :], Rb[:, :, 0, :], Fb[:, :, 1, mm - 1:mm].to_broadcast(shape), ALU.mult)\
                            .then_inc(s_decay, 1)
                        pool.wait_ge(s_decay, DECAY * h + 2 * level)
                        pool.tensor_tensor(Fb[:, :, 1, :], Fb[:, :, 1, :], Fb[:, :, 0, mm - 1:mm].to_broadcast(shape), ALU.mult)\
                            .then_inc(s_decay, 1)

            @block.vector
            def _(dve):
                dve.wait_ge(s_mask, 16)
                dve.wait_ge(s_zero, 5)
                with dve.Fori(0, HG_HEADS) as h:
                    dve.wait_ge(s_sig, 2 * h + 2)
                    dve.tensor_scalar(F[:, :], F[:, :], m.lb[:, 1, bass.ds(h, 1)], m.lb[:, 0, bass.ds(h, 1)], ALU.mult, ALU.add)\
                       .then_inc(s_gate, 1)
                    dve.wait_ge(s_gate, 2 * h + 1)
                    dve.tensor_scalar(k[:, :], F[:, :], -1.0, 1.0, ALU.mult, ALU.add).then_inc(s_gate, 1)
                    dve.wait_ge(s_q, 2 * h + 2)

                    def factors(level):
                        second = [blocks(t, level)[:, :, 1, :] for t in (Q[:, level % 2, :], q[:, :], F[:, :])]
                        if level == 1:
                            dve.wait_ge(s_o, 2 * h)
                            dve.tensor_tensor(*second, ALU.mult).then_inc(s_kq, 1)
                            return
                        dve.wait_ge(s_decay, DECAY * h + 1 + 2 * (level - 1))
                        if level >= 3:
                            dve.wait_ge(s_a, A * h + 2 * (level - 1))
                        first = [blocks(t, level)[:, :, 0, :] for t in (K[:, level % 2, :], k[:, :], R[:, :])]
                        dve.tensor_tensor(*first, ALU.mult).then_inc(s_kq, 1)
                        dve.tensor_tensor(*second, ALU.mult).then_inc(s_kq, 1)

                    def select(level):
                        for half in range(2):
                            i = 2 * level + half
                            if i >= 2:
                                dve.wait_ge(s_sel, A * h + i - 1)
                            wait_apart(dve, s_a, A * h + i + 1, s_apart)
                            dve.copy_predicated(AT[:, 4 * half:4 * half + 4, :],
                                                mask[:, level, :].unsqueeze(1).to_broadcast([P, 4, P]),
                                                work[i % 4][:, :].rearrange("p (c t) -> p c t", c=4)).then_inc(s_sel, 1)

                    for level in range(1, LEVELS + 1):
                        factors(level)
                        select(level - 1)
                    dve.wait_ge(s_decay, DECAY * (h + 1))
                    dve.wait_ge(s_a, A * h + 2 * LEVELS)
                    dve.tensor_tensor(K[:, 0, :], k[:, :], R[:, :], ALU.mult).then_inc(s_kq, 1)
                    dve.tensor_tensor(Q[:, 0, :], q[:, :], F[:, :], ALU.mult).then_inc(s_kq, 1)
                    select(LEVELS)
                    dve.wait_ge(s_kv, h + 1)
                    for c in range(1, TT):
                        kv = proj[2 + (c - 1) // 4][:, ((c - 1) % 4) * P:((c - 1) % 4 + 1) * P]
                        if c == 1:
                            dve.tensor_copy(S[:, c, :], kv).then_inc(s_state, 1)
                            continue
                        dve.wait_ge(s_state, STATE * h + c - 1)
                        dve.scalar_tensor_tensor(out=S[:, c, :], in0=S[:, c - 1, :], scalar=F[:, c * P - 1:c * P], in1=kv,
                                                 op0=ALU.mult, op1=ALU.add).then_inc(s_state, 1)


def recurrence_norm(nc, m, a):
    with Stage(nc, "hgrn_out") as st:
        norm = RmsNorm(st, m, SEQ)
        calls = [norm.plan(1, SEQ, P) for _ in range(HG_HEADS)]
        s_scaled, s_gated = st.sem("scaled"), st.sem("gated")
        with nc.Block() as block:
            @block.scalar
            def _(act):
                for h, k in enumerate(calls):
                    norm.square(act, k, lambda f: m.hgrnT[:, h, :])
                    norm.root(act, k)

            @block.tensor
            def _(pe):
                for h, k in enumerate(calls):
                    norm.total(pe, k)
                    pe.wait_ge(s_scaled, h)
                    norm.spread(pe, k)

            @block.vector
            def _(dve):
                at = VEC_C["hgrn_norm"]
                for h, k in enumerate(calls):
                    norm.invert(dve, k)
                    norm.wait_spread(dve, k)
                    dve.scalar_tensor_tensor(out=m.hgrnT[:, h, :], in0=m.hgrnT[:, h, :], scalar=m.vec[2][:, at:at + 1],
                                             in1=norm.rb[:, 0:SEQ], op0=ALU.mult, op1=ALU.mult).then_inc(s_scaled, 1)
                    dve.wait_ge(s_scaled, h + 1)
                    dve.tensor_tensor(m.hgrnT[:, h, :], m.hgrnT[:, h, :], m.silu_g[:, h, :], ALU.mult).then_inc(s_gated, 1)
                dve.wait_ge(s_gated, HG_HEADS)


def mix_branches(nc, m, a):
    ring = m.ring
    half_rows = QH // 2 * HD

    chunks = []
    for g in range(2):
        cols = slice(512 * g, 512 * g + 512)
        za = ring.plan((slot_cols(512), weight_cols(a["w_in_2"][0], 2816 + 512 * g, 2816 + 512 * g + 512)))
        zb = ring.plan((slot_cols(512), weight_cols(a["w_in_2"][0], 3840 + 512 * g, 3840 + 512 * g + 512)))
        parts = []
        for half in range(2):
            parts.append((lambda s, half=half: s[HD * half:HD * half + HD, 0:2048].rearrange("p (j c) -> p j c", j=4),
                          a["w_branch_attn_2"][0, half * half_rows:(half + 1) * half_rows, cols].rearrange("(j d) c -> d j c", d=HD)))
        parts.append((lambda s: s[:, 2048:4096].rearrange("p (j c) -> p j c", j=4),
                      a["w_branch_hgrn_2"][0, :, cols].rearrange("(j d) c -> d j c", d=P)))
        chunks.append((za, zb, ring.plan(*parts)))
    with Stage(nc, "mix") as st:
        sig, part = st.sb("sig", [P, 2, 2, BANK]), st.sb("part", [P, 2, 2, BANK])
        banks = [[st.ps(f"{n}{i}") for n in ("za", "zb", "ba", "bh")] for i in range(2)]
        s_mm, s_sig, s_part, s_mix = st.sem("product"), st.sem("sigmoid"), st.sem("part"), st.sem("mixed")
        with nc.Block() as block:
            @block.sync
            def _(sp):
                ring.send(sp, chunks[-1][-1])
                m.prefetch(sp)

            @block.tensor
            def _(pe):
                for i in range(2 * KT):
                    f, cols = i // 2, slice((i % 2) * BANK, (i % 2 + 1) * BANK)
                    if i % 8 == 0:
                        for chunk in chunks[f // 4]:
                            pe.wait_ge(*ring.landed_at(chunk))
                    za, zb, br = (ring.slot(chunk)[:, :].rearrange("p (k c) -> p k c", k=KT) for chunk in chunks[f // 4])
                    own = slice((f % 4) * P, (f % 4 + 1) * P)
                    if i >= 2:
                        pe.wait_ge(s_part, 2 * (i - 1))
                    for bank, w, src, lo, hi in ((0, za, m.aT, 0, KT), (1, zb, m.aT, 0, KT), (2, br, m.attnT, 0, 4),
                                                 (3, br, m.hgrnT, 4, KT)):
                        for k in range(lo, hi):
                            mm = pe.matmul(banks[i % 2][bank][:, :], w[:, k, own], src[:, k - lo, cols],
                                           start=(k == lo), stop=(k == hi - 1))
                        mm.then_inc(s_mm, 1)
                    if i % 8 == 7:
                        pe.wait_ge(s_mm, 4 * (i + 1))
                        pe.sem_inc(ring.used, 3)

            @block.scalar
            def _(act):
                for i in range(2 * KT):
                    for z in range(2):
                        act.wait_ge(s_mm, 4 * i + z + 1)
                        if i >= 2:
                            act.wait_ge(s_part, 2 * (i - 2) + z + 1)
                        act.activation(sig[:, i % 2, z, :], banks[i % 2][z][:, :], ACT.Sigmoid).then_inc(s_sig, 1)

            @block.vector
            def _(dve):
                for i in range(2 * KT):
                    f, cols = i // 2, slice((i % 2) * BANK, (i % 2 + 1) * BANK)
                    for z in range(2):
                        dve.wait_ge(s_mm, 4 * i + z + 3)
                        dve.wait_ge(s_sig, 2 * i + z + 1)
                        if i >= 2:
                            dve.wait_ge(s_mix, i - 1)
                        dve.tensor_tensor(part[:, i % 2, z, :], banks[i % 2][2 + z][:, :], sig[:, i % 2, z, :], ALU.mult)\
                           .then_inc(s_part, 1)
                    dve.wait_ge(s_part, 2 * i + 2)
                    dve.tensor_tensor(m.mixT[:, f, cols], part[:, i % 2, 0, :], part[:, i % 2, 1, :], ALU.add).then_inc(s_mix, 1)


def mixers(nc, m, a, ctx, out):
    with ExitStack() as c:
        m.attnT = c.enter_context(nc.sbuf_tensor("attnT", [P, 4, SEQ], F32))
        window_attention(nc, m, a)
        m.hgrnT = c.enter_context(nc.sbuf_tensor("hgrnT", [P, HG_HEADS, SEQ], F32))
        with ExitStack() as c2:
            m.silu_g = c2.enter_context(nc.sbuf_tensor("silu_g", [P, HG_HEADS, SEQ], F32))
            gated_recurrence(nc, m, a)
            recurrence_norm(nc, m, a)
        m.mixT = c.enter_context(nc.sbuf_tensor("mixT", [P, KT, SEQ], F32))
        m.prefetch = lambda sp: None
        mix_branches(nc, m, a)
        chunks = [m.ring.plan((slot_cols(512), weight_cols(a["w_out_2"][0], 512 * j, 512 * j + 512))) for j in range(2)]
        m.prefetch = lambda sp: m.ring.send(sp, chunks[-1])
        add_product(nc, m, chunks, m.mixT, "mix_out")


def route(nc, m, a, ctx, out):
    m.row_tok = ctx.enter_context(nc.sbuf_tensor("row_tok", [P, BLOCKS], U32))
    m.meta = ctx.enter_context(nc.sbuf_tensor("meta", [P, BLOCKS + 1], I32))
    m.dest = ctx.enter_context(nc.sbuf_tensor("dest", [P, 2, TT], U32))
    m.gate_w = ctx.enter_context(nc.sbuf_tensor("gate_w", [P, 2, TT], F32))
    m.hn_rows = nc.dram_tensor("hn_rows", (SEQ, D), F32, kind="Internal").ap()
    ROUTES = GROUPS + EXPERTS
    MAGIC = 1.5 * 2.0 ** 23
    FAR = 100.0
    m.x2 = m.aT[:, :, :].rearrange("p f t -> p (f t)").rearrange("p (t f) -> p t f", t=TT)
    with Stage(nc, "route") as st:
        norm = RmsNorm(st, m, SEQ)
        n_x = norm.plan(KT, SEQ, D)
        hn = st.sb("hn", [P, TT, D])
        w, bias = st.sb("w", [P, KT, ROUTES]), st.sb("bias", [P, ROUTES])
        iota, tok, tri = st.sb("iota", [P, P]), st.sb("tok", [P, TT]), st.sb("tri", [P, P])
        logit = st.sb("logit", [P, TT, ROUTES])
        gexp, geq = st.sb("gexp", [P, TT, GROUPS]), st.sb("geq", [P, TT, GROUPS])
        pick = st.sb("pick", [P, TT, PER_GROUP, GROUPS])
        eexp, eeq = st.sb("eexp", [P, TT, PER_GROUP]), st.sb("eeq", [P, TT, PER_GROUP])
        gtop, gsum, gsel, etop, esum = (st.sb(n, [P, TT]) for n in ("gtop", "gsum", "gsel", "etop", "esum"))
        val, eid, vsum = st.sb("val", [P, 2, TT]), st.sb("eid", [P, 2, TT]), st.sb("vsum", [P, TT])
        hot, both, place = st.sb("hot", [P, 2, TT, EXPERTS]), st.sb("both", [P, TT, EXPERTS]), st.sb("place", [P, TT, EXPERTS])
        spread = st.sb("spread", [P, TT, EXPERTS])
        count, blocks, upto = st.sb("count", [P, EXPERTS]), st.sb("blocks", [P, EXPERTS]), st.sb("upto", [P, 2, EXPERTS])
        dest, at_blk, at_row = st.sb("dest_f", [P, 2, TT]), st.sb("at_blk", [P, 2, TT]), st.sb("at_row", [P, 2, TT])
        hot_blk, hot_row = st.sb("hot_blk", [P, 2, TT, BLOCKS]), st.sb("hot_row", [P, 2, TT, P])
        owner, owner_n = st.sb("owner", [P, BLOCKS, EXPERTS]), st.sb("owner_n", [P, BLOCKS])
        tps = [st.ps(f"turn{i}") for i in range(4)]
        rps = st.ps("small")
        s_in, s_hn, s_logit, s_step, s_exp = (st.sem(n) for n in ("in", "hn", "logit", "step", "exp"))
        s_prefix, s_rows, s_turn, s_even, s_odd, s_out = (st.sem(n) for n in ("prefix", "rows", "turn", "even", "odd", "out"))
        mark = {}

        groups = []
        for src, dst in ((m.aT, hn), (m.xT, m.x2)):
            for t in range(TT):
                for half in range(2):
                    groups.append(([src[:, 4 * half + i, t * P:(t + 1) * P] for i in range(4)],
                                   dst[:, t, half * BANK:(half + 1) * BANK]))

        def evacuate(eng, copy, parity, done):
            for g in range(parity, len(groups), 2):
                eng.wait_ge(s_turn, g + 1)
                copy(groups[g][1], tps[g % 4][:, :]).then_inc(done, 1)

        with nc.Block() as block:
            @block.sync
            def _(sp):
                wr = w[:, :, :]
                sp.dma_start(wr[:, :, 0:GROUPS], a["w_router_group_2"][0].rearrange("(k p) c -> p k c", p=P)).then_inc(s_in, 16)
                sp.dma_start(wr[:, :, GROUPS:], a["w_router_expert_2"][0].rearrange("(k p) c -> p k c", p=P)).then_inc(s_in, 16)
                sp.dma_start(bias[:, 0:GROUPS], a["b_router_group_2"][0].partition_broadcast(P)).then_inc(s_in, 16)
                sp.dma_start(bias[:, GROUPS:], a["b_router_expert_2"][0].partition_broadcast(P)).then_inc(s_in, 16)
                sp.dma_start(iota[:, :], a["route_iota"]).then_inc(s_in, 16)
                sp.dma_start(tok[:, :], a["route_tok"]).then_inc(s_in, 16)
                sp.dma_start(tri[:, :], a["route_tri"]).then_inc(s_in, 16)
                for t in range(TT):
                    sp.wait_ge(s_even, t + 1)
                    sp.wait_ge(s_odd, t + 1)
                    sp.dma_start(m.hn_rows[t * P:(t + 1) * P, :], hn[:, t, :]).then_inc(s_out, 16)
                sp.wait_ge(s_out, 16 * TT)

            @block.vector
            def _(dve):
                norm.invert(dve, n_x)
                norm.wait_spread(dve, n_x)
                for f in range(KT):
                    at = VEC_C["norm2_w"] + f
                    dve.scalar_tensor_tensor(out=m.aT[:, f, :], in0=m.xT[:, f, :], scalar=m.vec[2][:, at:at + 1],
                                             in1=norm.rb[:, 0:SEQ], op0=ALU.mult, op1=ALU.mult).then_inc(s_hn, 1)
                steps = [0]

                def step(ins):
                    ins.then_inc(s_step, 1)
                    steps[0] += 1
                    dve.wait_ge(s_step, steps[0])

                def over(x, shape):
                    return x.unsqueeze(2).to_broadcast(shape)

                def row(n, shape):
                    return iota[:, 0:n].unsqueeze(1).to_broadcast(shape)

                def first_of(eq, n, dst):
                    shape = [P, TT, n]
                    step(dve.scalar_tensor_tensor(out=eq, in0=eq, scalar=-FAR, in1=row(n, shape), op0=ALU.mult, op1=ALU.add))
                    step(dve.tensor_reduce(dst, eq, AX.X, ALU.min))
                    step(dve.tensor_scalar(dst, dst, FAR, None, ALU.add))

                G, E = [P, TT, GROUPS], [P, TT, PER_GROUP]
                dve.wait_ge(s_in, 16 * 7)
                dve.wait_ge(s_logit, 1)
                step(dve.tensor_tensor(logit[:, :, :], rps[:, 0:TT * ROUTES].rearrange("p (t c) -> p t c", t=TT),
                                       bias[:, :].unsqueeze(1).to_broadcast([P, TT, ROUTES]), ALU.add))
                lg = logit[:, :, 0:GROUPS]
                step(dve.tensor_reduce(gtop[:, :], lg, AX.X, ALU.max))
                step(dve.tensor_tensor(gexp[:, :, :], lg, over(gtop[:, :], G), ALU.subtract))
                mark["groups"] = steps[0]
                dve.wait_ge(s_exp, 1)
                step(dve.tensor_reduce(gsum[:, :], gexp[:, :, :], AX.X, ALU.add))
                step(dve.reciprocal(gtop[:, :], gsum[:, :]))
                step(dve.tensor_tensor(gexp[:, :, :], gexp[:, :, :], over(gtop[:, :], G), ALU.mult))
                step(dve.tensor_reduce(gtop[:, :], gexp[:, :, :], AX.X, ALU.max))
                step(dve.tensor_tensor(geq[:, :, :], gexp[:, :, :], over(gtop[:, :], G), ALU.is_equal))
                first_of(geq[:, :, :], GROUPS, gsel[:, :])
                step(dve.tensor_tensor(geq[:, :, :], row(GROUPS, G), over(gsel[:, :], G), ALU.is_equal))
                step(dve.tensor_tensor(pick[:, :, :, :], logit[:, :, GROUPS:].rearrange("p t (g e) -> p t e g", g=GROUPS),
                                       geq[:, :, :].unsqueeze(2).to_broadcast([P, TT, PER_GROUP, GROUPS]), ALU.mult))
                step(dve.tensor_reduce(eexp[:, :, :], pick[:, :, :, :], AX.X, ALU.add))
                step(dve.tensor_reduce(etop[:, :], eexp[:, :, :], AX.X, ALU.max))
                step(dve.tensor_tensor(eexp[:, :, :], eexp[:, :, :], over(etop[:, :], E), ALU.subtract))
                mark["experts"] = steps[0]
                dve.wait_ge(s_exp, 2)
                step(dve.tensor_reduce(esum[:, :], eexp[:, :, :], AX.X, ALU.add))
                step(dve.reciprocal(etop[:, :], esum[:, :]))
                step(dve.tensor_tensor(eexp[:, :, :], eexp[:, :, :], over(etop[:, :], E), ALU.mult))
                for k in range(2):
                    step(dve.tensor_reduce(val[:, k, :], eexp[:, :, :], AX.X, ALU.max))
                    step(dve.tensor_tensor(eeq[:, :, :], eexp[:, :, :], over(val[:, k, :], E), ALU.is_equal))
                    first_of(eeq[:, :, :], PER_GROUP, eid[:, k, :])
                    if k == 0:
                        step(dve.tensor_tensor(eeq[:, :, :], row(PER_GROUP, E), over(eid[:, 0, :], E), ALU.is_equal))
                        step(dve.scalar_tensor_tensor(out=eexp[:, :, :], in0=eeq[:, :, :], scalar=-2.0, in1=eexp[:, :, :],
                                                      op0=ALU.mult, op1=ALU.add))
                step(dve.tensor_tensor(vsum[:, :], val[:, 0, :], val[:, 1, :], ALU.add))
                step(dve.reciprocal(esum[:, :], vsum[:, :]))
                for k in range(2):
                    step(dve.tensor_tensor(val[:, k, :], val[:, k, :], gtop[:, :], ALU.mult))
                    step(dve.tensor_tensor(m.gate_w[:, k, :], val[:, k, :], esum[:, :], ALU.mult))
                O = [P, TT, EXPERTS]
                for k in range(2):
                    step(dve.scalar_tensor_tensor(out=eid[:, k, :], in0=gsel[:, :], scalar=float(PER_GROUP), in1=eid[:, k, :],
                                                  op0=ALU.mult, op1=ALU.add))
                    step(dve.tensor_tensor(hot[:, k, :, :], row(EXPERTS, O), over(eid[:, k, :], O), ALU.is_equal))
                step(dve.tensor_tensor(both[:, :, :], hot[:, 0, :, :], hot[:, 1, :, :], ALU.add))
                mark["both"] = steps[0]
                dve.wait_ge(s_prefix, 1)
                W = TT * EXPERTS
                step(dve.tensor_copy(spread[:, :, :].rearrange("p t e -> p (t e)"), rps[:, W:2 * W]))
                step(dve.tensor_copy(place[:, :, :].rearrange("p t e -> p (t e)"), rps[:, 0:W]))
                mark["prefix"] = steps[0]
                step(dve.tensor_copy(count[:, :], spread[:, 0, :]))
                for t in range(1, TT):
                    step(dve.tensor_tensor(place[:, t, :], place[:, t, :], count[:, :], ALU.add))
                    step(dve.tensor_tensor(count[:, :], count[:, :], spread[:, t, :], ALU.add))
                step(dve.tensor_scalar(blocks[:, :], count[:, :], (P - 1) / 2.0, 1.0 / P, ALU.add, ALU.mult))
                step(dve.tensor_scalar(blocks[:, :], blocks[:, :], MAGIC, None, ALU.add))
                step(dve.tensor_scalar(blocks[:, :], blocks[:, :], MAGIC, None, ALU.subtract))
                step(dve.tensor_copy(upto[:, 0, :], blocks[:, :]))
                for i in range(5):
                    s, d, n = upto[:, i % 2, :], upto[:, 1 - i % 2, :], 1 << i
                    step(dve.tensor_copy(d[:, 0:n], s[:, 0:n]))
                    step(dve.tensor_tensor(d[:, n:], s[:, n:], s[:, 0:EXPERTS - n], ALU.add))
                ends = upto[:, 1, :]
                step(dve.tensor_tensor(blocks[:, :], ends, blocks[:, :], ALU.subtract))
                step(dve.scalar_tensor_tensor(out=place[:, :, :], in0=blocks[:, :].unsqueeze(1).to_broadcast(O), scalar=float(P),
                                              in1=place[:, :, :], op0=ALU.mult, op1=ALU.add))
                for k in range(2):
                    step(dve.tensor_tensor(spread[:, :, :], hot[:, k, :, :], place[:, :, :], ALU.mult))
                    step(dve.tensor_reduce(dest[:, k, :], spread[:, :, :], AX.X, ALU.add))
                step(dve.tensor_copy(m.dest[:, :, :], dest[:, :, :]))
                step(dve.tensor_scalar(at_blk[:, :, :], dest[:, :, :], -(P - 1) / 2.0, 1.0 / P, ALU.add, ALU.mult))
                step(dve.tensor_scalar(at_blk[:, :, :], at_blk[:, :, :], MAGIC, None, ALU.add))
                step(dve.tensor_scalar(at_blk[:, :, :], at_blk[:, :, :], MAGIC, None, ALU.subtract))
                step(dve.scalar_tensor_tensor(out=at_row[:, :, :], in0=at_blk[:, :, :], scalar=-float(P), in1=dest[:, :, :],
                                              op0=ALU.mult, op1=ALU.add))
                for k in range(2):
                    B, R = [P, TT, BLOCKS], [P, TT, P]
                    step(dve.tensor_tensor(hot_blk[:, k, :, :], row(BLOCKS, B), over(at_blk[:, k, :], B), ALU.is_equal))
                    step(dve.tensor_tensor(hot_blk[:, k, :, :], hot_blk[:, k, :, :], over(tok[:, :], B), ALU.mult))
                    step(dve.tensor_tensor(hot_row[:, k, :, :], row(P, R), over(at_row[:, k, :], R), ALU.is_equal))
                mark["hot"] = steps[0]
                B = [P, BLOCKS, EXPERTS]
                step(dve.tensor_tensor(owner[:, :, :], ends.unsqueeze(1).to_broadcast(B), over(iota[:, 0:BLOCKS], B), ALU.is_le))
                step(dve.tensor_reduce(owner_n[:, :], owner[:, :, :], AX.X, ALU.add))
                step(dve.tensor_scalar(owner_n[:, :], owner_n[:, :], EXPERTS - 1.0, None, ALU.min))
                step(dve.tensor_copy(m.meta[:, 0:BLOCKS], owner_n[:, :]))
                step(dve.tensor_copy(m.meta[:, BLOCKS:BLOCKS + 1], ends[:, EXPERTS - 1:EXPERTS]))
                dve.wait_ge(s_rows, 1)
                step(dve.tensor_copy(m.row_tok[:, :], rps[:, 0:BLOCKS]))
                evacuate(dve, lambda o, i: dve.tensor_copy(o, i), 0, s_even)

            @block.tensor
            def _(pe):
                norm.total(pe, n_x)
                norm.spread(pe, n_x)
                pe.wait_ge(s_hn, KT)
                pe.wait_ge(s_in, 16 * 7)
                for t in range(TT):
                    for k in range(KT):
                        mm = pe.matmul(rps[:, t * ROUTES:(t + 1) * ROUTES], m.aT[:, k, t * P:(t + 1) * P], w[:, k, :],
                                       start=(k == 0), stop=(k == KT - 1))
                mm.then_inc(s_logit, 1)

                def turn(lo, hi):
                    for g in range(lo, hi):
                        if g >= 4:
                            pe.wait_ge(s_odd if g % 2 else s_even, (g - 4) // 2 + 1)
                        for i, src in enumerate(groups[g][0]):
                            mm = pe.transpose(tps[g % 4][:, i * P:(i + 1) * P], src, m.ident[:, :])
                        mm.then_inc(s_turn, 1)

                turn(0, 4)
                W = TT * EXPERTS
                pe.wait_ge(s_step, mark["both"])
                flat = both[:, :, :].rearrange("p t e -> p (t e)")
                pe.matmul(rps[:, 0:W], tri[:, :], flat, start=True, stop=True)
                pe.matmul(rps[:, W:2 * W], m.ones[:, :], flat, start=True, stop=True).then_inc(s_prefix, 1)
                pe.wait_ge(s_step, mark["hot"])
                for k in range(2):
                    for t in range(TT):
                        mm = pe.matmul(rps[:, 0:BLOCKS], hot_row[:, k, t, :], hot_blk[:, k, t, :],
                                       start=(k == 0 and t == 0), stop=(k == 1 and t == TT - 1))
                mm.then_inc(s_rows, 1)
                turn(4, len(groups))

            @block.scalar
            def _(act):
                norm.square(act, n_x, lambda f: m.xT[:, f, :])
                norm.root(act, n_x)
                for name, x in (("groups", gexp), ("experts", eexp)):
                    act.wait_ge(s_step, mark[name])
                    act.activation(x[:, :, :], x[:, :, :], ACT.Exp).then_inc(s_exp, 1)
                evacuate(act, lambda o, i: act.activation(o, i, ACT.Copy), 1, s_odd)


def experts(nc, m, a, ctx, out):
    m.y_rows = nc.dram_tensor("y_rows", (BLOCKS * P, D), F32, kind="Internal").ap()
    KF = FF // P
    flat_x = m.xT[:, :, :].rearrange("p f t -> p (f t)")
    with Stage(nc, "moe") as st:
        spare = st.sb("w_spare", [P, 4096])
        rooms = [m.ring.slots[0][:, :], m.ring.slots[1][:, :], m.ring.slots[2][:, :],
                 flat_x[:, 0:4096], flat_x[:, 4096:8192], spare[:, :]]
        wg, wu, wd = ([rooms[3 * b + i].rearrange("p (k c) -> p k c", k=n) for b in range(2)]
                      for i, n in enumerate((KT, KT, KF)))
        idx = st.sb("idx", [P, 2], U32)
        x = [st.sb(f"x{b}", [P, D]) for b in range(2)]
        xT, gate, h, hT = st.sb("xT", [P, 2, KT, P]), st.sb("gate", [P, FF]), st.sb("h", [P, FF]), st.sb("hT", [P, KF, P])
        y, blank = st.sb("y", [P, 2, D]), st.sb("blank", [P, D])
        xp = [st.ps(f"xp{i}") for i in range(2)]
        gp, upp, hp = st.ps("gp"), st.ps("up"), st.ps("hp")
        yp = [st.ps(f"yp{i}") for i in range(2)]
        s_wg, s_wu, s_wd, s_x, s_stored = ([st.sem(f"{n}{b}") for b in range(2)] for n in ("wg", "wu", "wd", "x", "stored"))
        s_g, s_u, s_y = ([st.sem(f"{n}{b}") for b in range(2)] for n in ("g", "u", "y"))
        s_idx, s_xp, s_xa, s_xv = (st.sem(n) for n in ("idx", "x_turned", "x_act", "x_dve"))
        s_silu, s_h, s_hp, s_hT, s_ya, s_yv = (st.sem(n) for n in ("silu", "h", "h_turned", "hT", "y_act", "y_dve"))
        s_apart, s_blank, s_blanked = st.sem("apart"), st.sem("blank"), st.sem("blanked")

        def in_use(eng):
            return eng.value_load(m.meta[0:1, BLOCKS:BLOCKS + 1], min_val=1, max_val=BLOCKS)

        with nc.Block() as block:
            @block.sync
            def _(sp):
                used = in_use(sp)
                with sp.Fori(0, BLOCKS // 2) as pair:
                    for b in range(2):
                        n = 2 * pair + b
                        with sp.If(n < used):
                            e = sp.value_load(m.meta[0:1, bass.ds(n, 1)], min_val=0, max_val=EXPERTS - 1)
                            sp.wait_ge(s_g[b], pair)
                            sp.dma_start(wg[b], a["w_gate_experts_2"][0, bass.ds(e, 1)].rearrange("o (p k) c -> p (o k) c", k=KT))\
                              .then_inc(s_wg[b], 16)
                            sp.wait_ge(s_u[b], pair)
                            sp.dma_start(wu[b], a["w_up_experts_2"][0, bass.ds(e, 1)].rearrange("o (p k) c -> p (o k) c", k=KT))\
                              .then_inc(s_wu[b], 16)
                            sp.wait_ge(s_y[b], 2 * pair)
                            sp.dma_start(wd[b], a["w_down_experts_2"][0, bass.ds(e, 1)].rearrange("o (p k) c -> p (o k) c", k=KF))\
                              .then_inc(s_wd[b], 16)

            @block.gpsimd
            def _(pool):
                used = in_use(pool)
                with pool.Fori(0, BLOCKS // 2) as pair:
                    for b in range(2):
                        n = 2 * pair + b
                        with pool.If(n < used):
                            wait_apart(pool, s_xp, 4 * pair, s_apart)
                            pool.tensor_copy(idx[:, b:b + 1], m.row_tok[:, bass.ds(n, 1)]).then_inc(s_idx, 1)
                            wait_apart(pool, s_idx, n + 1, s_apart)
                            pool.indirect_dma_start(x[b][:, :], None, m.hn_rows,
                                                    bass.IndirectOffsetOnAxis(idx[:, b:b + 1], 0)).then_inc(s_x[b], 16)
                pool.memset(blank[:, :], 0.0).then_inc(s_blank, 1)
                pool.wait_ge(s_blank, 1)
                with pool.Fori(0, BLOCKS) as n:
                    with pool.If(n + used < BLOCKS):
                        pool.dma_start(m.y_rows[bass.ds((BLOCKS - 1 - n) * P, P), :], blank[:, :]).then_inc(s_blanked, 16)
                        with pool.If(n + used + 1 >= BLOCKS):
                            wait_apart(pool, s_blanked, 16 * n + 16, s_apart)

            @block.tensor
            def _(pe):
                used = in_use(pe)

                def turn_rows(n, pair, b):
                    pe.wait_ge(s_x[b], 16 * pair + 16)
                    pe.wait_ge(s_xa, n)
                    pe.wait_ge(s_xv, n)
                    for k in range(KT):
                        mm = pe.transpose(xp[k // 4][:, (k % 4) * P:(k % 4 + 1) * P], x[b][:, k:D:KT], m.ident[:, :])
                        if k % 4 == 3:
                            mm.then_inc(s_xp, 1)

                turn_rows(0, 0, 0)
                with pe.Fori(0, BLOCKS // 2) as pair:
                    for b in range(2):
                        n = 2 * pair + b
                        with pe.If(n < used):
                            pe.wait_ge(s_xa, n + 1)
                            pe.wait_ge(s_xv, n + 1)
                            pe.wait_ge(s_h, n)
                            pe.wait_ge(s_wg[b], 16 * pair + 16)
                            for k in range(KT):
                                mm = pe.matmul(gp[:, :], xT[:, b, k, :], wg[b][:, k, :], start=(k == 0), stop=(k == KT - 1))
                            mm.then_inc(s_g[b], 1)
                            pe.wait_ge(s_wu[b], 16 * pair + 16)
                            for k in range(KT):
                                mm = pe.matmul(upp[:, :], xT[:, b, k, :], wu[b][:, k, :], start=(k == 0), stop=(k == KT - 1))
                            mm.then_inc(s_u[b], 1)
                            with pe.If(n + 1 < used):
                                turn_rows(n + 1, pair + b, 1 - b)
                            pe.wait_ge(s_h, n + 1)
                            pe.wait_ge(s_hT, n)
                            for k in range(KF):
                                mm = pe.transpose(hp[:, k * P:(k + 1) * P], h[:, k:FF:KF], m.ident[:, :])
                            mm.then_inc(s_hp, 1)
                            pe.wait_ge(s_hT, n + 1)
                            pe.wait_ge(s_ya, n)
                            pe.wait_ge(s_yv, n)
                            pe.wait_ge(s_wd[b], 16 * pair + 16)
                            for half in range(2):
                                for k in range(KF):
                                    mm = pe.matmul(yp[half][:, :], hT[:, k, :], wd[b][:, k, half * BANK:(half + 1) * BANK],
                                                   start=(k == 0), stop=(k == KF - 1))
                                mm.then_inc(s_y[b], 1)

            @block.scalar
            def _(act):
                used = in_use(act)

                def rows_out(n, b):
                    act.wait_ge(s_xp, 2 * n + 1)
                    act.activation(xT[:, b, 0:4, :].rearrange("p k t -> p (k t)"), xp[0][:, :], ACT.Copy).then_inc(s_xa, 1)

                rows_out(0, 0)
                with act.Fori(0, BLOCKS // 2) as pair:
                    for b in range(2):
                        n = 2 * pair + b
                        with act.If(n < used):
                            act.wait_ge(s_g[b], pair + 1)
                            act.wait_ge(s_h, n)
                            act.activation(gate[:, :], gp[:, :], ACT.Silu).then_inc(s_silu, 1)
                            with act.If(n + 1 < used):
                                rows_out(n + 1, 1 - b)
                            act.wait_ge(s_y[b], 2 * pair + 1)
                            act.wait_ge(s_stored[b], 16 * pair)
                            act.activation(y[:, b, 0:BANK], yp[0][:, :], ACT.Copy).then_inc(s_ya, 1)
                            act.wait_ge(s_ya, n + 1)
                            act.wait_ge(s_yv, n + 1)
                            act.dma_start(m.y_rows[bass.ds(n * P, P), :], y[:, b, :]).then_inc(s_stored[b], 16)
                            with act.If(n + 1 >= used):
                                wait_apart(act, s_stored[b], 16 * pair + 16, s_apart)
                                wait_apart(act, s_stored[1 - b], 16 * (pair + b), s_apart)

            @block.vector
            def _(dve):
                used = in_use(dve)

                def rows_out(n, b):
                    dve.wait_ge(s_xp, 2 * n + 2)
                    dve.tensor_copy(xT[:, b, 4:8, :].rearrange("p k t -> p (k t)"), xp[1][:, :]).then_inc(s_xv, 1)

                rows_out(0, 0)
                with dve.Fori(0, BLOCKS // 2) as pair:
                    for b in range(2):
                        n = 2 * pair + b
                        with dve.If(n < used):
                            dve.wait_ge(s_u[b], pair + 1)
                            dve.wait_ge(s_silu, n + 1)
                            dve.wait_ge(s_hp, n)
                            dve.tensor_tensor(h[:, :], gate[:, :], upp[:, :], ALU.mult).then_inc(s_h, 1)
                            with dve.If(n + 1 < used):
                                rows_out(n + 1, 1 - b)
                            dve.wait_ge(s_y[1 - b], 2 * (pair + b))
                            dve.wait_ge(s_hp, n + 1)
                            dve.tensor_copy(hT[:, :, :].rearrange("p k t -> p (k t)"), hp[:, :]).then_inc(s_hT, 1)
                            dve.wait_ge(s_y[b], 2 * pair + 2)
                            dve.wait_ge(s_stored[b], 16 * pair)
                            dve.tensor_copy(y[:, b, BANK:D], yp[1][:, :]).then_inc(s_yv, 1)


def combine(nc, m, a, ctx, out):
    with Stage(nc, "combine") as st:
        rooms = [m.ring.slots[i][:, j * D:(j + 1) * D] for i in range(3) for j in range(4)]
        s_row = [st.sem(f"row{i}") for i in range(2 * TT)]
        s_sum, s_out = st.sem("sum"), st.sem("out")
        with nc.Block() as block:
            @block.gpsimd
            def _(pool):
                for i in range(2 * TT):
                    t, k = i // 2, i % 2
                    if i >= len(rooms):
                        pool.wait_ge(s_sum, i - len(rooms) + 1)
                    pool.indirect_dma_start(rooms[i % len(rooms)], None, m.y_rows,
                                            bass.IndirectOffsetOnAxis(m.dest[:, k, t:t + 1], 0)).then_inc(s_row[i], 16)

            @block.vector
            def _(dve):
                for i in range(2 * TT):
                    t, k = i // 2, i % 2
                    dve.wait_ge(s_row[i], 16)
                    if k:
                        dve.wait_ge(s_sum, i)
                    dve.scalar_tensor_tensor(out=m.x2[:, t, :], in0=rooms[i % len(rooms)], scalar=m.gate_w[:, k, t:t + 1],
                                             in1=m.x2[:, t, :], op0=ALU.mult, op1=ALU.add).then_inc(s_sum, 1)

            @block.sync
            def _(sp):
                for t in range(TT):
                    sp.wait_ge(s_sum, 2 * t + 2)
                    sp.dma_start(out[0, t * P:(t + 1) * P, :], m.x2[:, t, :]).then_inc(s_out, 16)
                sp.wait_ge(s_out, 16 * TT)


STAGES = [mla_layer, hyena_layer, second_norms, mixers, route, experts, combine]


def program(nc, a, out, stages):
    with ExitStack() as ctx:
        def sb(name, shape, dt=F32):
            return ctx.enter_context(nc.sbuf_tensor(name, shape, dt))

        m = Names()
        m.ident, m.ones = sb("ident", [P, P]), sb("ones", [P, P])
        m.vec = [sb(f"vec{i}", [P, 96]) for i in range(3)]
        m.cond = sb("cond", [P, KT, 2])
        m.ada = sb("ada", [P, 2, 24, 2])
        m.gain = sb("gain", [P, 2, 2, KT])
        m.xT = sb("xT", [P, KT, SEQ])
        slots = [sb(f"ring{i}", [P, 4096]) for i in range(3)]
        m.ring = Ring(slots, [ctx.enter_context(nc.semaphore(f"ring_loaded{i}")) for i in range(3)],
                      ctx.enter_context(nc.semaphore("ring_used")))
        for stage in stages:
            stage(nc, m, a, ctx, out)


INPUTS = [
    "x", "c", "ctx", "c_ctx", "norm_g", "ada_w", "ada_b", "final_g", "mla_w_in", "mla_q_norm_g",
    "mla_kv_norm_g", "mla_w_uq", "mla_w_ukv", "mla_w_out", "hy_w_in", "hy_conv_w", "hy_conv_b",
    "hy_filt_w_in", "hy_filt_w_hid", "hy_filt_b", "hy_filt_freq", "hy_filt_w_out", "hy_bias", "hy_w_out",
    "positions_2", "norm1_w_2", "w_in_2", "q_norm_w_2", "k_norm_w_2", "attn_sinks_2",
    "hgrn_lower_bounds_2", "hgrn_norm_w_2", "w_branch_attn_2", "w_branch_hgrn_2", "w_out_2", "norm2_w_2",
    "w_router_group_2", "b_router_group_2", "w_router_expert_2", "b_router_expert_2", "w_gate_experts_2",
    "w_up_experts_2", "w_down_experts_2",
]


def build(nc, shapes, stages=len(STAGES)):
    a = {name: nc.dram_tensor(f"in_{name}", shape, dtype, kind="ExternalInput").ap()
         for name, (shape, dtype) in shapes.items()}
    out = nc.dram_tensor("out", (1, SEQ, D), F32, kind="ExternalOutput").ap()
    program(nc, a, out, STAGES[:stages])


def kernel(**inputs):
    import concourse.bacc as bacc
    from concourse.bass_utils import run_bass_kernel_spmd

    nc = bacc.Bacc("TRN2", target_bir_lowering=False, num_devices=1)
    arrays = {name: np.ascontiguousarray(inputs[name]) for name in INPUTS}
    arrays.update(constants())
    build(nc, {n: (v.shape, mybir.dt.from_np(v.dtype)) for n, v in arrays.items()})
    result = run_bass_kernel_spmd(nc, [{f"in_{n}": v for n, v in arrays.items()}], core_ids=[0])
    return result.results[0]["out"]
```
